# Optimizing a Trainium2 kernel written in Bass

```python
import jax, jax.numpy as jnp
from jax import lax
import numpy as np

D_MODEL = 1024
BATCH = 1
SEQ = 256
DEPTH = 2

HEAD_DIM = 64
RMS_EPS = 1e-6
Q_BLOCK = 128
SPARSE_Q_BLOCK = 64
MLA_HEADS = 8
MLA_NOPE = 64
MLA_ROPE = 32
MLA_QK = MLA_NOPE + MLA_ROPE
MLA_V = 64
MLA_Q_RANK = 768
MLA_KV_RANK = 256
ROPE_THETA = 10000.0
MOBA_HEADS = 4
MOBA_BLOCK = 256
MOBA_TOPK = 3
DSA_HEADS = 4
IDX_HEADS = 16
IDX_DIM = 32
DSA_TOPK = 256
D_FF = -(-8 * D_MODEL // (3 * 256)) * 256
IN_WIDTHS = (MLA_Q_RANK, MLA_KV_RANK, MLA_ROPE,
             3 * MOBA_HEADS * HEAD_DIM, 3 * DSA_HEADS * HEAD_DIM,
             IDX_HEADS * IDX_DIM, IDX_DIM, IDX_HEADS, 3 * D_MODEL)
N_IN = sum(IN_WIDTHS)

kernel_name = "hybrid_mla_moba_dsa_gated_block"

def rms_norm(x, g, eps=RMS_EPS):
    xf = x.astype(jnp.float32)
    y = xf * lax.rsqrt(jnp.mean(xf * xf, axis=-1, keepdims=True) + eps)
    return (y * g.astype(jnp.float32)).astype(x.dtype)

def alibi_slopes(n):
    return jnp.asarray([2.0 ** (-8.0 * (i + 1) / n) for i in range(n)], dtype=jnp.float32)

def apply_rope(x, pos):
    half = x.shape[-1] // 2
    freqs = ROPE_THETA ** (-jnp.arange(half, dtype=jnp.float32) / half)
    ang = pos.astype(jnp.float32)[:, None] * freqs[None, :]
    cos, sin = jnp.cos(ang), jnp.sin(ang)
    x1 = x[..., :half].astype(jnp.float32)
    x2 = x[..., half:].astype(jnp.float32)
    return jnp.concatenate([x1 * cos - x2 * sin, x1 * sin + x2 * cos], -1).astype(x.dtype)

def split_columns(proj):
    outs, start = [], 0
    for wdt in IN_WIDTHS:
        outs.append(proj[..., start:start + wdt])
        start += wdt
    return outs

def dense_causal_attention(q, k, v):
    B, H, S, Dqk = q.shape
    scale = Dqk ** -0.5
    kpos = jnp.arange(S)

    def one(i):
        start = i * Q_BLOCK
        qi = lax.dynamic_slice_in_dim(q, start, Q_BLOCK, axis=2)
        qpos = start + jnp.arange(Q_BLOCK)
        s = jnp.einsum('bhqd,bhkd->bhqk', qi, k, preferred_element_type=jnp.float32) * scale
        s = jnp.where(kpos[None, :] <= qpos[:, None], s, -jnp.inf)
        p = jax.nn.softmax(s, axis=-1).astype(v.dtype)
        return jnp.einsum('bhqk,bhkd->bhqd', p, v)

    out = lax.map(one, jnp.arange(S // Q_BLOCK))
    return out.transpose(1, 2, 0, 3, 4).reshape(B, H, S, v.shape[-1])

def moba_attention(q, k, v, slopes):
    B, H, S, Dh = q.shape
    nb = -(-S // MOBA_BLOCK)
    pad = nb * MOBA_BLOCK - S
    k_pad = jnp.pad(k, ((0, 0), (0, 0), (0, pad), (0, 0)))
    v_pad = jnp.pad(v, ((0, 0), (0, 0), (0, pad), (0, 0)))
    kb = k_pad.reshape(B, H, nb, MOBA_BLOCK, Dh)
    vb = v_pad.reshape(B, H, nb, MOBA_BLOCK, Dh)
    k_mean = jnp.mean(kb.astype(jnp.float32), axis=3)
    n_sel = max(1, min(MOBA_TOPK, nb - 1))
    scale = Dh ** -0.5
    slope = slopes[None, :, None, None]
    bi = jnp.arange(B)[:, None, None, None]
    hi = jnp.arange(H)[None, :, None, None]
    blk_off = jnp.arange(MOBA_BLOCK)
    n_keys_sel = n_sel * MOBA_BLOCK

    def one(i):
        start = i * SPARSE_Q_BLOCK
        qi = lax.dynamic_slice_in_dim(q, start, SPARSE_Q_BLOCK, axis=2)
        qpos = start + jnp.arange(SPARSE_Q_BLOCK)
        own = start // MOBA_BLOCK
        k_own = lax.dynamic_slice_in_dim(k_pad, own * MOBA_BLOCK, MOBA_BLOCK, axis=2)
        v_own = lax.dynamic_slice_in_dim(v_pad, own * MOBA_BLOCK, MOBA_BLOCK, axis=2)
        kpos_own = own * MOBA_BLOCK + blk_off
        s_own = (jnp.einsum('bhqd,bhkd->bhqk', qi, k_own, preferred_element_type=jnp.float32) * scale
                 - slope * (qpos[:, None] - kpos_own[None, :]).astype(jnp.float32))
        s_own = jnp.where(kpos_own[None, :] <= qpos[:, None], s_own, -jnp.inf)
        gate = jnp.einsum('bhqd,bhnd->bhqn', qi.astype(jnp.float32), k_mean)
        gate = jnp.where(jnp.arange(nb) < own, gate, -jnp.inf)
        _, idx = lax.top_k(gate, n_sel)
        valid = jnp.repeat(idx < own, MOBA_BLOCK, axis=-1)
        k_sel = kb[bi, hi, idx].reshape(B, H, SPARSE_Q_BLOCK, n_keys_sel, Dh)
        v_sel = vb[bi, hi, idx].reshape(B, H, SPARSE_Q_BLOCK, n_keys_sel, Dh)
        kpos_sel = (idx[..., None] * MOBA_BLOCK + blk_off).reshape(B, H, SPARSE_Q_BLOCK, n_keys_sel)
        s_sel = (jnp.einsum('bhqd,bhqkd->bhqk', qi, k_sel, preferred_element_type=jnp.float32) * scale
                 - slope * (qpos[:, None] - kpos_sel).astype(jnp.float32))
        s_sel = jnp.where(valid, s_sel, -jnp.inf)
        p = jax.nn.softmax(jnp.concatenate([s_sel, s_own], axis=-1), axis=-1).astype(v.dtype)
        return (jnp.einsum('bhqk,bhqkd->bhqd', p[..., :n_keys_sel], v_sel)
                + jnp.einsum('bhqk,bhkd->bhqd', p[..., n_keys_sel:], v_own))

    out = lax.map(one, jnp.arange(S // SPARSE_Q_BLOCK))
    return out.transpose(1, 2, 0, 3, 4).reshape(B, H, S, Dh)

def dsa_attention(q, k, v, iq, ik, iw, slopes):
    B, H, S, Dh = q.shape
    n_keep = min(DSA_TOPK, S // 4)
    scale = Dh ** -0.5
    idx_scale = (IDX_DIM * IDX_HEADS) ** -0.5
    slope = slopes[None, :, None, None]
    kpos = jnp.arange(S)
    bi = jnp.arange(B)[:, None, None]

    def one(i):
        start = i * SPARSE_Q_BLOCK
        qpos = start + jnp.arange(SPARSE_Q_BLOCK)
        qi = lax.dynamic_slice_in_dim(q, start, SPARSE_Q_BLOCK, axis=2)
        iqi = lax.dynamic_slice_in_dim(iq, start, SPARSE_Q_BLOCK, axis=1)
        iwi = lax.dynamic_slice_in_dim(iw, start, SPARSE_Q_BLOCK, axis=1)
        dots = jnp.einsum('bqhd,bsd->bqhs', iqi, ik, preferred_element_type=jnp.float32)
        score = jnp.einsum('bqhs,bqh->bqs', jax.nn.relu(dots), iwi.astype(jnp.float32)) * idx_scale
        score = jnp.where(kpos[None, None, :] <= qpos[None, :, None], score, -jnp.inf)
        _, idx = lax.top_k(score, n_keep)
        valid = idx <= qpos[None, :, None]
        k_sel = k[bi, idx]
        v_sel = v[bi, idx]
        s = (jnp.einsum('bhqd,bqkhd->bhqk', qi, k_sel, preferred_element_type=jnp.float32) * scale
             - slope * (qpos[None, None, :, None] - idx[:, None]).astype(jnp.float32))
        s = jnp.where(valid[:, None], s, -jnp.inf)
        p = jax.nn.softmax(s, axis=-1).astype(v.dtype)
        return jnp.einsum('bhqk,bqkhd->bhqd', p, v_sel)

    out = lax.map(one, jnp.arange(S // SPARSE_Q_BLOCK))
    return out.transpose(1, 2, 0, 3, 4).reshape(B, H, S, Dh)

def token_mixer(h, w_in, g_cq, w_uq, g_ckv, w_ukv, qn_mla, kn_mla, qn_moba, kn_moba,
                qn_dsa, kn_dsa, w_br_a, w_br_b, w_br_c, w_out):
    B, S, _ = h.shape
    pos = jnp.arange(S)
    slopes = alibi_slopes(MOBA_HEADS + DSA_HEADS)
    proj = jnp.einsum('bsd,dn->bsn', h, w_in)
    cq, ckv, kr, qkv_b, qkv_c, iq, ik, iw, gate_logits = split_columns(proj)

    q_a = jnp.einsum('bsr,rn->bsn', rms_norm(cq, g_cq), w_uq).reshape(B, S, MLA_HEADS, MLA_QK)
    kv_a = jnp.einsum('bsr,rn->bsn', rms_norm(ckv, g_ckv), w_ukv).reshape(B, S, MLA_HEADS, MLA_NOPE + MLA_V)
    k_a = jnp.concatenate(
        [kv_a[..., :MLA_NOPE], jnp.broadcast_to(kr[:, :, None, :], (B, S, MLA_HEADS, MLA_ROPE))], axis=-1)
    v_a = kv_a[..., MLA_NOPE:].transpose(0, 2, 1, 3)
    q_a = rms_norm(q_a, qn_mla).transpose(0, 2, 1, 3)
    k_a = rms_norm(k_a, kn_mla).transpose(0, 2, 1, 3)
    q_a = jnp.concatenate([q_a[..., :MLA_NOPE], apply_rope(q_a[..., MLA_NOPE:], pos)], axis=-1)
    k_a = jnp.concatenate([k_a[..., :MLA_NOPE], apply_rope(k_a[..., MLA_NOPE:], pos)], axis=-1)
    y_a = dense_causal_attention(q_a, k_a, v_a).transpose(0, 2, 1, 3).reshape(B, S, MLA_HEADS * MLA_V)
    y_a = jnp.einsum('bsk,kd->bsd', y_a, w_br_a)

    qkv_b = qkv_b.reshape(B, S, 3, MOBA_HEADS, HEAD_DIM)
    q_b = rms_norm(qkv_b[:, :, 0], qn_moba).transpose(0, 2, 1, 3)
    k_b = rms_norm(qkv_b[:, :, 1], kn_moba).transpose(0, 2, 1, 3)
    v_b = qkv_b[:, :, 2].transpose(0, 2, 1, 3)
    y_b = moba_attention(q_b, k_b, v_b, slopes[0::2]).transpose(0, 2, 1, 3).reshape(B, S, MOBA_HEADS * HEAD_DIM)
    y_b = jnp.einsum('bsk,kd->bsd', y_b, w_br_b)

    qkv_c = qkv_c.reshape(B, S, 3, DSA_HEADS, HEAD_DIM)
    q_c = rms_norm(qkv_c[:, :, 0], qn_dsa).transpose(0, 2, 1, 3)
    k_c = rms_norm(qkv_c[:, :, 1], kn_dsa)
    v_c = qkv_c[:, :, 2]
    y_c = dsa_attention(q_c, k_c, v_c, iq.reshape(B, S, IDX_HEADS, IDX_DIM), ik, iw, slopes[1::2])
    y_c = jnp.einsum('bsk,kd->bsd', y_c.transpose(0, 2, 1, 3).reshape(B, S, DSA_HEADS * HEAD_DIM), w_br_c)

    g_a, g_b, g_c = jnp.split(jax.nn.sigmoid(gate_logits), 3, axis=-1)
    merged = g_a * y_a + g_b * y_b + g_c * y_c
    return jnp.einsum('bsd,de->bse', merged, w_out)

def swiglu(h, w_gu, w_down):
    gu = jnp.einsum('bsd,df->bsf', h, w_gu)
    g, u = jnp.split(gu, 2, axis=-1)
    return jnp.einsum('bsf,fd->bsd', jax.nn.silu(g) * u, w_down)

def setup_inputs(seed: int = 0) -> dict:
    key = jax.random.key(seed)
    ks = iter(jax.random.split(key, 32))
    L, D = DEPTH, D_MODEL

    def w(shape, fan_in):
        return jax.random.normal(next(ks), shape, jnp.float32) * fan_in ** -0.5

    def gain(n):
        return 1.0 + 0.02 * jax.random.normal(next(ks), (L, n), jnp.float32)

    return {
        "x": jax.random.normal(next(ks), (BATCH, SEQ, D), jnp.float32),
        "c": jax.random.normal(next(ks), (BATCH, D), jnp.float32),
        "w_ada": w((L, D, 6 * D), D),
        "b_ada": 0.02 * jax.random.normal(next(ks), (L, 6 * D), jnp.float32),
        "norm1": gain(D),
        "w_in": w((L, D, N_IN), D),
        "g_cq": gain(MLA_Q_RANK),
        "w_uq": w((L, MLA_Q_RANK, MLA_HEADS * MLA_QK), MLA_Q_RANK),
        "g_ckv": gain(MLA_KV_RANK),
        "w_ukv": w((L, MLA_KV_RANK, MLA_HEADS * (MLA_NOPE + MLA_V)), MLA_KV_RANK),
        "qn_mla": gain(MLA_QK),
        "kn_mla": gain(MLA_QK),
        "qn_moba": gain(HEAD_DIM),
        "kn_moba": gain(HEAD_DIM),
        "qn_dsa": gain(HEAD_DIM),
        "kn_dsa": gain(HEAD_DIM),
        "w_br_a": w((L, MLA_HEADS * MLA_V, D), MLA_HEADS * MLA_V),
        "w_br_b": w((L, MOBA_HEADS * HEAD_DIM, D), MOBA_HEADS * HEAD_DIM),
        "w_br_c": w((L, DSA_HEADS * HEAD_DIM, D), DSA_HEADS * HEAD_DIM),
        "w_out": w((L, D, D), D),
        "norm2": gain(D),
        "w_gu": w((L, D, 2 * D_FF), D),
        "w_down": w((L, D_FF, D), D_FF),
    }

def reference(x, c, w_ada, b_ada, norm1, w_in, g_cq, w_uq, g_ckv, w_ukv, qn_mla, kn_mla,
              qn_moba, kn_moba, qn_dsa, kn_dsa, w_br_a, w_br_b, w_br_c, w_out, norm2, w_gu, w_down):
    cond = jax.nn.silu(c)
    for l in range(DEPTH):
        mod = jnp.einsum('bd,dn->bn', cond, w_ada[l]) + b_ada[l]
        sh1, sc1, g1, sh2, sc2, g2 = [m[:, None, :] for m in jnp.split(mod, 6, axis=-1)]
        h = rms_norm(x, norm1[l]) * (1.0 + sc1) + sh1
        x = x + g1 * token_mixer(h, w_in[l], g_cq[l], w_uq[l], g_ckv[l], w_ukv[l], qn_mla[l], kn_mla[l],
                                 qn_moba[l], kn_moba[l], qn_dsa[l], kn_dsa[l],
                                 w_br_a[l], w_br_b[l], w_br_c[l], w_out[l])
        h = rms_norm(x, norm2[l]) * (1.0 + sc2) + sh2
        x = x + g2 * swiglu(h, w_gu[l], w_down[l])
    return x


_drawn_inputs = setup_inputs


def setup_inputs(seed=0):
    import zlib

    import numpy as np

    out = dict(_drawn_inputs(seed))
    spreads = {}
    factors = {'g_cq': 8.0,
     'g_ckv': 7.176,
     'qn_mla': 8.0,
     'kn_mla': 8.0,
     'qn_moba': 8.0,
     'kn_moba': 7.447,
     'qn_dsa': 8.0,
     'kn_dsa': 8.0}
    for name, (base, spread) in spreads.items():
        noise = np.random.default_rng([zlib.crc32(name.encode()), seed]).standard_normal(out[name].shape)
        drawn = base * np.exp(spread * noise) if base else spread * noise
        out[name] = __import__('jax').numpy.asarray(drawn.astype(out[name].dtype))
    for name, factor in factors.items():
        out[name] = (out[name] * factor).astype(out[name].dtype)
    return out
```

```python
from contextlib import ExitStack

import numpy as np

import concourse.bass as bass
from concourse import mybir
from concourse.bass import ds

F32 = mybir.dt.float32
F32R = mybir.dt.float32r
ALU = mybir.AluOpType
ACT = mybir.ActivationFunctionType
AX_X = mybir.AxisListType.X

P = 128
D = 1024
T = 256
DEPTH = 2
KT = D // P
TT = T // P
HD = 64
EPS = 1e-6
ROPE_THETA = 10000.0

A_HEADS, A_NOPE, A_ROPE, A_QK, A_V = 8, 64, 32, 96, 64
Q_RANK, KV_RANK = 768, 256
B_HEADS = C_HEADS = 4
IDX_HEADS, IDX_DIM = 16, 32
N_KEEP = min(256, T // 4)
D_FF = -(-8 * D // (3 * 256)) * 256

C_CKV = Q_RANK
C_KR = C_CKV + KV_RANK
C_B = C_KR + A_ROPE
C_C = C_B + 3 * B_HEADS * HD
C_IQ = C_C + 3 * C_HEADS * HD
C_IK = C_IQ + IDX_HEADS * IDX_DIM
C_IW = C_IK + IDX_DIM
C_G = C_IW + IDX_HEADS
C_BV = C_B + 2 * B_HEADS * HD
C_CV = C_C + 2 * C_HEADS * HD

RING = 3
SLAB = 2048
CHUNKS = 8
CW = C_G // CHUNKS
KGRP = [(0, 3), (3, 3), (6, 2)]
S_GATE0 = CHUNKS * len(KGRP)
S_UQ = S_GATE0 + 6
S_UKV = S_UQ + 3
S_GATE1 = S_UKV + 1
S_BR = S_GATE1 + 6
S_OUT = S_BR + 4
S_FF = S_OUT + 4
FG = D_FF // 256
NS = S_FF + 3 * FG
S_FFL = S_FF + 5
FF_PAIRS = (FG - 3) // 2
S_FFE = S_FFL + 6 * FF_PAIRS
NEG = -1.0e30
TAKEN = -3.0e38
IDX_SCALE = float((IDX_DIM * IDX_HEADS) ** -0.5)
SLOPES = [2.0 ** (-8.0 * (i + 1) / (B_HEADS + C_HEADS)) for i in range(B_HEADS + C_HEADS)]
ADA_T0, ADA_TN = 2 * D, 3 * D
ROWS = 48 + 8 + 8 + 6 + 2 + 8
R_N1, R_N2, R_GQ, R_GKV, R_C = 48, 56, 64, 70, 72

K_ID = 0
K_CM = K_ID + P
K_ND = K_CM + P + T
K_COS = K_ND + P + T
K_SIN = K_COS + TT * A_ROPE
K_FAC = K_SIN + TT * A_ROPE
K_ALL = K_FAC + 2 * TT * 2 * B_HEADS


def constants():
    t = np.zeros((P, K_ALL), np.float32)
    t[:, K_ID:K_ID + P] = np.eye(P)
    for tok in range(TT):
        q = tok * P + np.arange(P)[:, None]
        k = np.arange(P * (tok + 1))[None, :]
        at = tok * P
        t[:, K_CM + at:K_CM + at + k.size] = np.where(k <= q, 0.0, NEG)
        t[:, K_ND + at:K_ND + at + k.size] = np.where(k <= q, -(q - k), NEG)
        half = A_ROPE // 2
        freqs = np.float32(ROPE_THETA) ** (-np.arange(half, dtype=np.float32) / np.float32(half))
        ang = q.astype(np.float32) * freqs[None, :].astype(np.float32)
        cos, sin = np.cos(ang), np.sin(ang)
        t[:, K_COS + tok * A_ROPE:K_COS + (tok + 1) * A_ROPE] = np.concatenate([cos, cos], 1)
        t[:, K_SIN + tok * A_ROPE:K_SIN + (tok + 1) * A_ROPE] = np.concatenate([-sin, sin], 1)
        for kind in range(2):
            for h in range(B_HEADS):
                t[:, K_FAC + kind * 16 + tok * 8 + h] = HD ** -0.5 / SLOPES[2 * h + kind]
                t[:, K_FAC + kind * 16 + tok * 8 + 4 + h] = 1.0
    return t


class Event:

    def __init__(self, sem, per_layer, start=0):
        self.sem, self.per_layer, self.start = sem, per_layer, start

    def at(self, l, n):
        return l * self.per_layer + (n + self.start)


class Chain:

    def __init__(self, eng, event, l):
        self.eng, self.event, self.l, self.n = eng, event, l, 0

    def __call__(self, ins):
        ins.then_inc(self.event.sem, 1)
        self.n += 1
        self.eng.wait_ge(self.event.sem, self.event.at(self.l, self.n))


def slab_words(s):
    if s < S_GATE0:
        return KGRP[s % 3][1] * CW
    return 2 * Q_RANK if S_UQ <= s < S_UKV else SLAB


def gate_bank(g):
    return g % 3 if g < 6 else g % 2


def raw_level(s):
    two = [S_BR + 1, S_BR + 3] + [S_FF + k for k in range(NS - S_FF) if k < 4 or (k < 31 and k % 3 != 1)]
    return 16 * sum(2 if n in two else 1 for n in range(s % RING, s + 1, RING))


HEADS = [("b", h) for h in range(B_HEADS)] + [("a", h) for h in range(A_HEADS)] + [("c", h) for h in range(C_HEADS)]
NH = len(HEADS)


def head_slope(kind, h):
    return 1.0 if kind == "a" else SLOPES[2 * h + (kind == "c")]


PAIR_Y = [4, 5, 0, 1, 2, 3, 6, 7]
GATE_AT = {1: 2, 5: 3, 9: 4, 13: 5}
DVE_LINKS = 103
ACT_LINKS = 6


def build(nc, x, c, w_ada, b_ada, norm1, w_in, g_cq, w_uq, g_ckv, w_ukv, qn_mla, kn_mla, qn_moba, kn_moba,
          qn_dsa, kn_dsa, w_br_a, w_br_b, w_br_c, w_out, norm2, w_gu, w_down, const, out):
    with ExitStack() as ctx:
        def sb(name, shape, dt=F32):
            return ctx.enter_context(nc.sbuf_tensor(name, shape, dt))

        def event(name, per_layer, start=0):
            return Event(ctx.enter_context(nc.semaphore(name)), per_layer, start)

        raw = sb("raw", [P, RING, SLAB])
        w_hi = sb("w_hi", [P, RING, SLAB], F32R)
        w_lo = sb("w_lo", [P, RING, SLAB], F32R)
        x_t = sb("x_t", [P, KT, T])
        h_hi = sb("h_hi", [P, KT, T], F32R)
        h_lo = sb("h_lo", [P, KT, T], F32R)
        proj = sb("proj", [P, TT, C_G])
        y_hi = sb("y_hi", [P, KT, T], F32R)
        y_lo = sb("y_lo", [P, KT, T], F32R)
        front = sb("front", [P, 2 * A_HEADS + 4 + 12, T])
        kz_t = sb("kz_t", [P, 8, T])
        acc = sb("acc", [P, 3072])
        ikz = sb("ikz", [P, 4, T])
        score = sb("score", [P, P + T])
        sel_nd = sb("sel_nd", [P, P + T])
        konst = sb("konst", [P, K_ALL])
        gains = sb("gains", [P, 2 * A_QK + 4 * HD])
        cols = sb("cols", [P, DEPTH, ROWS])
        ones = sb("ones", [P, P])
        rstd = sb("rstd", [P, T])
        cond = sb("cond", [P, KT])
        cond_now = sb("cond_now", [P, 2])
        mod_b = sb("mod_b", [P, 24])
        mod_a = sb("mod_a", [P, 24])
        pcol = sb("pcol", [P, ROWS])
        small = sb("small", [P, 96])
        krr = sb("krr", [P, TT, A_ROPE])
        krw = sb("krw", [P, TT, A_ROPE])

        eps = small[:, 0:1]
        ssc = small[:, 1:5]
        krss = small[:, 5:7]
        rowmax = [small[:, 8 + 8 * i:10 + 8 * i] for i in range(2)]
        negmax = [small[:, 10 + 8 * i:12 + 8 * i] for i in range(2)]
        rowsum = [small[:, 12 + 8 * i:14 + 8 * i] for i in range(2)]
        rinv = [small[:, 14 + 8 * i:16 + 8 * i] for i in range(2)]
        top8 = small[:, 24:32]
        ss16 = small[:, 32:48]
        fac16 = small[:, 48:64]
        ss16b = small[:, 64:80]

        qk_t = front[:, 0:16, :]
        pq_t = front[:, 16:20, :]
        own = front[:, 20:32, :].rearrange("p a b -> p (a b)")
        sq = acc[:, 0:1536]
        mod_rows_sb = acc[:, 0:1024]
        relu_b = [acc[:, 1536 + 384 * i:1536 + 384 * (i + 1)] for i in range(4)]
        p_sb = [acc[:, 1536 + 384 * i:1536 + 384 * (i + 1)] for i in range(2)]
        pt_sb = [acc[:, 2304 + 384 * i:2304 + 384 * (i + 1)] for i in range(2)]
        q_a = own[:, 0:1536]
        k_a = own[:, 1536:3072]
        iq_t = own[:, 2048:3072].rearrange("p (j t) -> p j t", j=4)
        ik_rep = rstd[:, :].rearrange("p (t m) -> p t m", t=TT)
        ada_raw = [front[:, 12 * i:12 * (i + 1), :].rearrange("p a b -> p (a b)") for i in range(2)]
        ada_pro = [qk_t[:, 0:8, :].rearrange("p a b -> p (a b)"), qk_t[:, 8:16, :].rearrange("p a b -> p (a b)"),
                   own[:, 0:2048]]
        vrows = proj[0:ROWS, 0, 2048:2048 + DEPTH * P].rearrange("r (l m) -> r l m", l=DEPTH)
        ident = konst[:, K_ID:K_ID + P]
        causal = konst[:, K_CM:K_CM + P + T]
        neg_dist = konst[:, K_ND:K_ND + P + T]
        k_nope = proj[:, :, 0:1024].rearrange("p t (h e) -> p t h e", h=A_HEADS)[:, :, :, 0:A_NOPE]
        silu_g = [proj[:, 0, 512 * i:512 * (i + 1)] for i in range(2)]
        glu = [proj[:, 1, 512 * i:512 * (i + 1)] for i in range(2)]
        yh, yl = y_hi[:, :, :].rearrange("p a b -> p (a b)"), y_lo[:, :, :].rearrange("p a b -> p (a b)")
        glu_hi = [yh[:, 512 * i:512 * (i + 1)] for i in range(2)]
        glu_lo = [yl[:, 512 * i:512 * (i + 1)] for i in range(2)]

        def norm_pair(p):
            at = 1024 + (p % 2) * 512
            return proj[:, p // 2, at:at + 512]

        def merged(hf):
            return proj[:, hf, 0:1024]

        def gate(g):
            if g < 6:
                at = [C_IQ, 1024, C_C][g // 2]
                return proj[:, g % 2, at:at + 512]
            return own[:, (g - 6) * 512:(g - 5) * 512]

        bank = [ctx.enter_context(nc.psum_tensor(f"bank{i}", [P, 512], F32)) for i in range(8)]

        x_in = event("x_in", 0)
        konst_in = event("konst_in", 0)
        vrows_in = event("vrows_in", 0)
        ones_ok = event("ones_ok", 0)
        zeros_ok = event("zeros_ok", 0)
        x_tp = event("x_tp", 0)
        cols_tp = event("cols_tp", 0)
        cols_ok = event("cols_ok", 0)
        cond_done = event("cond_done", 0)
        apro_in = [event(f"apro_in{i}", 0) for i in range(3)]
        raw_in = [event(f"raw_in{i}", raw_level(NS - RING + i)) for i in range(RING)]
        gains_in = event("gains_in", 16 * 6)
        hi_ready = event("hi_ready", NS)
        lo_ready = event("lo_ready", NS, RING)
        slab_used = event("slab_used", NS, RING)
        ada_in = [event(f"ada_in{i}", 16 * 4 + 32 * 4) for i in range(2)]
        ada_used = event("ada_used", 16, KT)
        acc_zero = event("acc_zero", 2, 1)
        cond_ok = event("cond_ok", 8)
        x_done = event("x_done", 16, 8)
        sq_done = event("sq_done", 8)
        ss_done = event("ss_done", 2)
        std_done = event("std_done", 2)
        hn_done = event("hn_done", 8)
        hhi_done = event("hhi_done", 16)
        hlo_done = event("hlo_done", 8)
        coef_done = event("coef_done", 2)
        chunk_out = event("chunk_out", 2 * CHUNKS, 4)
        ikrep_done = event("ikrep_done", 2)
        idx_tp = event("idx_tp", 1)
        iqt_done = event("iqt_done", 2)
        ikz_done = event("ikz_done", 4)
        nd_done = event("nd_done", 1)
        mod_rows = event("mod_rows", 2, 1)
        mod_rows_out = event("mod_rows_out", 4, 2)
        mod_tp = event("mod_tp", 2, 1)
        mod_got = event("mod_got", 2, 1)
        cq_tp = event("cq_tp", 1)
        cq_hi = event("cq_hi", 8)
        cq_lo = event("cq_lo", 8)
        cq_ss = event("cq_ss", 4)
        cq_std = event("cq_std", 2)
        cq_rstd = event("cq_rstd", 1)
        idx_sc = event("idx_sc", IDX_HEADS)
        relu_done = event("relu_done", IDX_HEADS)
        idx_acc = event("idx_acc", 2 * IDX_HEADS)
        kr_done = event("kr_done", 1)
        psq_done = event("psq_done", 2)
        pss_done = event("pss_done", 2)
        pstd_done = event("pstd_done", 2)
        pn_done = event("pn_done", 2)
        pair_tp = event("pair_tp", 2)
        pq_out = event("pq_out", 2)
        kz_out = event("kz_out", 4)
        gate_out = event("gate_out", 12)
        uq_out = event("uq_out", 4)
        ukv_out = event("ukv_out", 4)
        msq_done = event("msq_done", 2)
        mss_done = event("mss_done", 2)
        mstd_done = event("mstd_done", 2)
        mqk_done = event("mqk_done", 2)
        mla_tp = event("mla_tp", 2)
        mla_out_a = event("mla_out_a", 4)
        mla_out_d = event("mla_out_d", 4)
        scored = event("scored", NH)
        maxed = event("maxed", NH)
        ttr_done = event("ttr_done", 2 * NH)
        exped = event("exped", 2 * NH)
        p_ready = event("p_ready", NH)
        p_tp = event("p_tp", NH)
        pt_out = event("pt_out", NH)
        pv_done = event("pv_done", NH)
        y_hi_done = event("y_hi_done", NH // 2)
        y_lo_done = event("y_lo_done", NH // 2)
        m_done = event("m_done", 4)
        m_hi = event("m_hi", 4)
        m_lo = event("m_lo", 4)
        silu_done = event("silu_done", FG)
        glu_done = event("glu_done", FG, 1)
        glu_hi_done = event("glu_hi_done", FG)
        glu_lo_done = event("glu_lo_done", FG)
        dve_pro = event("dve_pro", 0)
        dve_chain = event("dve_chain", DVE_LINKS)
        act_chain = event("act_chain", ACT_LINKS)
        out_tp = event("out_tp", 0)
        out_rows = event("out_rows", 0)
        out_stored = event("out_stored", 0)
        waited = event("waited", 0)

        block = ctx.enter_context(nc.Block())

        def apart(eng):
            eng.sem_inc(waited.sem, 1)

        @block.sync
        def _(sp):
            sp.dma_start(konst[:], const).then_inc(konst_in.sem, 16)
            for l in range(DEPTH):
                for src, at, n in ((b_ada, 0, 48), (norm1, R_N1, 8), (norm2, R_N2, 8), (g_cq, R_GQ, 6),
                                   (g_ckv, R_GKV, 2)):
                    sp.dma_start(vrows[at:at + n, l, :], src[l].rearrange("(r m) -> r m", m=P)).then_inc(vrows_in.sem, 16)
                sp.dma_start(vrows[R_C:R_C + 8, l, :], c[0].rearrange("(r m) -> r m", m=P)).then_inc(vrows_in.sem, 16)
            sp.dma_start(proj[:, :, 0:D], x[0].rearrange("(t p) d -> p t d", p=P)).then_inc(x_in.sem, 16)
            for k in range(KT):
                if k >= 3:
                    sp.wait_ge(ada_used.sem, k - 2)
                sp.dma_start(ada_pro[k % 3], w_ada[0, k * P:(k + 1) * P, 0:2 * D]).then_inc(apro_in[k % 3].sem, 16)
            with sp.Fori(0, DEPTH) as l:
                def load(s0, step, *parts):
                    sp.wait_ge(lo_ready.sem, lo_ready.at(l, step + (s0 + 1 - RING)))
                    apart(sp)
                    for dst, src in parts:
                        sp.dma_start(dst, src).then_inc(raw_in[s0 % RING].sem, 16)

                def rows(w, k0, k, c0, n):
                    return w.rearrange("l (c p) n -> l p c n", p=P)[l, :, k0:k0 + k, ds(c0, n)]

                def slot_view(s0, k, n, at=0):
                    return raw[:, s0 % RING, at:at + k * n].rearrange("p (c n) -> p c n", c=k)

                def chunk_pair(i):
                    for cc in range(2):
                        for j, (k0, k) in enumerate(KGRP):
                            load(3 * cc + j, 6 * i, (slot_view(j, k, CW), rows(
                                w_in, k0, k, (CHUNKS - 1 - cc) * CW - 2 * CW * i, CW)))

                with sp.Fori(0, CHUNKS // 2 - 1) as i:
                    chunk_pair(i)
                sp.wait_ge(coef_done.sem, coef_done.at(l, 1))
                apart(sp)
                at = 0
                for src, n in ((qn_mla, A_QK), (kn_mla, A_QK), (qn_moba, HD), (kn_moba, HD), (qn_dsa, HD),
                               (kn_dsa, HD)):
                    sp.dma_start(gains[:, at:at + n], src[l].partition_broadcast(P)).then_inc(gains_in.sem, 16)
                    at += n
                chunk_pair(CHUNKS // 2 - 1)

                def load_gates(s, g):
                    load(s, 0, (slot_view(s, KT, 256), rows(w_in, 0, KT, C_G + 256 * g, 256)))

                for g in range(6):
                    load_gates(S_GATE0 + g, g)
                for j in range(3):
                    load(S_UQ + j, 0, (slot_view(S_UQ + j, 2, Q_RANK), rows(w_uq, 2 * j, 2, 0, Q_RANK)))
                load(S_UKV, 0, (slot_view(S_UKV, 2, D), rows(w_ukv, 0, 2, 0, D)))
                for g in range(6, 12):
                    load_gates(S_GATE1 + g - 6, g)
                for hf in range(2):
                    s = S_BR + 2 * hf
                    load(s, 0, (slot_view(s, 4, 512), rows(w_br_a, 0, 4, 512 * hf, 512)))
                    load(s + 1, 0, (slot_view(s + 1, 2, 512), rows(w_br_b, 0, 2, 512 * hf, 512)),
                         (slot_view(s + 1, 2, 512, 1024), rows(w_br_c, 0, 2, 512 * hf, 512)))
                for o in range(4):
                    load(S_OUT + o, 0, (slot_view(S_OUT + o, KT, 256), rows(w_out, 0, KT, 256 * o, 256)))

                def load_gu(s0, step, i):
                    for kg in range(2):
                        v = raw[:, (s0 + kg) % RING, :].rearrange("p (c e n) -> p c e n", c=4, e=2)
                        load(s0 + kg, step, (v[:, :, 0, :], rows(w_gu, 4 * kg, 4, 256 * i, 256)),
                             (v[:, :, 1, :], rows(w_gu, 4 * kg, 4, 256 * i + D_FF, 256)))

                def load_down(s0, step, i):
                    load(s0, step, (slot_view(s0, 2, D), w_down.rearrange("l (c p) n -> l p c n", p=P)[l, :, ds(2 * i, 2), :]))

                load_gu(S_FF, 0, 0)
                load_gu(S_FF + 2, 0, 1)
                load_down(S_FF + 4, 0, 0)
                with sp.Fori(0, FF_PAIRS) as b:
                    for e in range(2):
                        load_gu(S_FFL + 3 * e, 6 * b, 2 * b + (e + 2))
                        load_down(S_FFL + 3 * e + 2, 6 * b, 2 * b + (e + 1))
                load_gu(S_FFE, 0, FG - 1)
                load_down(S_FFE + 2, 0, FG - 2)
                load_down(S_FFE + 3, 0, FG - 1)

            sp.wait_ge(out_rows.sem, 4)
            sp.dma_start(out[0].rearrange("(t p) d -> p t d", p=P), proj[:, :, 0:D]).then_inc(out_stored.sem, 16)
            sp.wait_ge(out_stored.sem, 16)

        @block.gpsimd
        def _(pool):
            nc.gpsimd.memset(ones[:], 1.0).then_inc(ones_ok.sem, 1)
            nc.gpsimd.memset(acc[:], 0.0).then_inc(acc_zero.sem, 1)
            nc.gpsimd.memset(eps, EPS).then_inc(zeros_ok.sem, 1)
            nc.gpsimd.memset(kz_t[:], 0.0).then_inc(zeros_ok.sem, 1)
            nc.gpsimd.memset(ikz[:], 0.0).then_inc(zeros_ok.sem, 1)
            pool.wait_ge(ada_used.sem, KT)
            with pool.Fori(0, DEPTH) as l:
                def load_ada(m, e, *parts):
                    pool.wait_ge(ada_used.sem, ada_used.at(l, m - 1))
                    apart(pool)
                    for dst, src in parts:
                        pool.dma_start(dst, src).then_inc(ada_in[e].sem, 16)

                pool.wait_ge(mod_tp.sem, mod_tp.at(l, 0))
                apart(pool)
                nc.gpsimd.memset(acc[:], 0.0).then_inc(acc_zero.sem, 1)
                with pool.Fori(0, KT // 2) as i:
                    for e in range(2):
                        load_ada(2 * i + e, e, (ada_raw[e], w_ada[l, ds(P * (2 * i + e), P), ADA_T0:ADA_T0 + ADA_TN]))
                pool.wait_ge(pv_done.sem, pv_done.at(l, NH))
                apart(pool)
                nc.gpsimd.memset(acc[:], 0.0).then_inc(acc_zero.sem, 1)
                pool.wait_ge(m_done.sem, m_done.at(l, 4))
                apart(pool)
                nxt = (l + 1) % DEPTH
                with pool.Fori(0, KT // 2) as i:
                    for e in range(2):
                        k = 2 * i + e
                        load_ada(k + KT, e, (ada_raw[e][:, 0:D], w_ada[l, ds(P * k, P), 5 * D:6 * D]),
                                 (ada_raw[e][:, D:3 * D], w_ada[nxt, ds(P * k, P), 0:2 * D]))

        @block.tensor
        def _(pe):
            pe.wait_ge(konst_in.sem, 16)
            pe.wait_ge(vrows_in.sem, 16 * 6 * DEPTH)
            for l in range(DEPTH):
                last = nc.tensor.transpose(bank[4][:, l * ROWS:(l + 1) * ROWS], vrows[:, l, :], ident[0:ROWS, 0:ROWS])
            last.then_inc(cols_tp.sem, 1)
            pe.wait_ge(x_in.sem, 16)
            for k in range(KT):
                for t in range(TT):
                    at = (k % 2) * T + t * P
                    last = nc.tensor.transpose(bank[k // 2][:, at:at + P], proj[:, t, k * P:(k + 1) * P], ident)
                if k % 2:
                    last.then_inc(x_tp.sem, 1)
            pe.wait_ge(ones_ok.sem, 1)
            pe.sem_inc(slab_used.sem, RING)

            def mod_columns(l, n, mods, used):
                pe.wait_ge(ada_used.sem, used)
                for j in range(6):
                    b, q = 6 + j // 4, 32 * (j % 4)
                    last = nc.tensor.matmul(bank[b][q:q + 32, :], ones[:, 0:32], acc[:, 512 * j:512 * (j + 1)],
                                            start=True, stop=True)
                last.then_inc(mod_rows.sem, 1)
                pe.wait_ge(mod_rows_out.sem, mods)
                for b in range(4):
                    nc.tensor.transpose(bank[6][:, P * b:P * (b + 1)], mod_rows_sb[:, P * b:P * (b + 1)], ident)
                for b in range(4):
                    last = nc.tensor.transpose(bank[7][:, 64 * b:64 * (b + 1)],
                                               mod_rows_sb[0:64, 512 + P * b:512 + P * (b + 1)], ident[0:64, 0:64])
                last.then_inc(mod_tp.sem, 1)

            mod_columns(0, 0, 2, KT)

            def slab(l, s0, step=0):
                pe.wait_ge(lo_ready.sem, lo_ready.at(l, step + (s0 + 1)))

            def passes(b_out, st, mv, st_hi, st_lo, mv_hi, mv_lo, start, stop):
                nc.tensor.matmul(b_out, st_hi, mv_hi, start=start, stop=False, skip_group_check=True)
                nc.tensor.matmul(b_out, st_hi, mv_lo, start=False, stop=False, skip_group_check=True)
                return nc.tensor.matmul(b_out, st_lo, mv_hi, start=False, stop=stop, skip_group_check=True)

            def channel_slab(s0, tiles, first, final):
                slot = s0 % RING
                for o, col, offs, act_hi, act_lo, opens in tiles:
                    for n, off in enumerate(offs):
                        last = passes(o, None, None, w_hi[:, slot, off + col:off + col + P],
                                      w_lo[:, slot, off + col:off + col + P], act_hi[n], act_lo[n],
                                      first and opens and n == 0, final and n == len(offs) - 1)
                return last

            def norm_sums(l, which, b):
                for p in range(4):
                    pe.wait_ge(sq_done.sem, sq_done.at(l, 4 * which + p + 1))
                    for e in range(2):
                        last = nc.tensor.matmul(bank[b][:, 0:T], ones[:, :], norm_pair(p)[:, e * T:(e + 1) * T],
                                                start=(p == 0 and e == 0), stop=(p == 3 and e == 1))
                last.then_inc(ss_done.sem, 1)

            def chunks(l, i, which):
                for cc in which:
                    pe.wait_ge(chunk_out.sem, chunk_out.at(l, 4 * i + (2 * cc + 2 - 4)))
                    for j, (k0, n) in enumerate(KGRP):
                        pe.wait_ge(hlo_done.sem, hlo_done.at(l, (k0 + n + 1) // 2))
                        slab(l, 3 * cc + j, 6 * i)
                        for t in range(TT):
                            for kk in range(n):
                                k = k0 + kk
                                hh, hl = h_hi[:, k, t * P:(t + 1) * P], h_lo[:, k, t * P:(t + 1) * P]
                                wh = w_hi[:, j, kk * CW:(kk + 1) * CW]
                                wl = w_lo[:, j, kk * CW:(kk + 1) * CW]
                                o = bank[2 * cc + t][:, 0:CW]
                                nc.tensor.matmul(o, hh, wh, start=(k == 0), stop=False)
                                nc.tensor.matmul(o, hl, wh, start=False, stop=False)
                                last = nc.tensor.matmul(o, hh, wl, start=False, stop=(k == KT - 1))
                        last.then_inc(slab_used.sem, 1)

            def gate_slab(l, g):
                s = S_GATE0 + g if g < 6 else S_GATE1 + g - 6
                slab(l, s)
                if 3 <= g < 6 or g >= 8:
                    pe.wait_ge(gate_out.sem, gate_out.at(l, g - 2 if g < 6 else g - 1))
                hi, lo = [h_hi[:, k, :] for k in range(KT)], [h_lo[:, k, :] for k in range(KT)]
                channel_slab(s, [(bank[gate_bank(g)][:, m * T:(m + 1) * T], m * P, [256 * k for k in range(KT)], hi, lo, m == 0)
                                 for m in range(2)], True, True).then_inc(slab_used.sem, 1)

            def token_slab(l, s, n_k, k0, width, n_chunk, cw, b0, first, final):
                slot = s % RING
                for t in range(TT):
                    for ch in range(n_chunk):
                        for kk in range(n_k):
                            a_hi = y_hi[:, k0 + kk, t * P:(t + 1) * P]
                            a_lo = y_lo[:, k0 + kk, t * P:(t + 1) * P]
                            at = kk * width + ch * cw
                            o = bank[b0 + n_chunk * t + ch][:, 0:cw]
                            nc.tensor.matmul(o, a_hi, w_hi[:, slot, at:at + cw], start=(first and kk == 0), stop=False)
                            nc.tensor.matmul(o, a_lo, w_hi[:, slot, at:at + cw], start=False, stop=False)
                            last = nc.tensor.matmul(o, a_hi, w_lo[:, slot, at:at + cw], start=False,
                                                    stop=(final and kk == n_k - 1))
                last.then_inc(slab_used.sem, 1)

            with pe.Fori(0, DEPTH) as l:
                norm_sums(l, 0, 4)
                with pe.Fori(0, CHUNKS // 2 - 1) as i:
                    chunks(l, i, (0, 1))
                chunks(l, CHUNKS // 2 - 1, (0,))

                pe.wait_ge(ikrep_done.sem, ikrep_done.at(l, 2))
                pe.wait_ge(chunk_out.sem, chunk_out.at(l, 12))
                for j in range(4):
                    for t in range(TT):
                        at = (j % 2) * T + t * P
                        nc.tensor.transpose(bank[4 + j // 2][:, at:at + P],
                                            proj[:, t, C_IQ + j * P:C_IQ + (j + 1) * P], ident)
                for t in range(TT):
                    last = nc.tensor.transpose(bank[6][:, t * P:(t + 1) * P], ik_rep[:, t, :], ident)
                last.then_inc(idx_tp.sem, 1)

                chunks(l, CHUNKS // 2 - 1, (1,))

                pe.wait_ge(ikz_done.sem, ikz_done.at(l, 4))
                mod_columns(l, 1, mod_rows_out.at(l, 2), ada_used.at(l, KT))

                pe.wait_ge(chunk_out.sem, chunk_out.at(l, 2 * CHUNKS))
                for k in range(KT):
                    for t in range(TT):
                        at = (k % 2) * T + t * P
                        last = nc.tensor.transpose(bank[k // 2][:, at:at + P], proj[:, t, k * P:(k + 1) * P], ident)
                last.then_inc(cq_tp.sem, 1)
                pe.wait_ge(cq_lo.sem, cq_lo.at(l, KT))
                gate_slab(l, 0)
                gate_slab(l, 1)

                pe.wait_ge(iqt_done.sem, iqt_done.at(l, 2))
                pe.wait_ge(mod_got.sem, mod_got.at(l, 1))
                for h in range(IDX_HEADS):
                    if h >= 4:
                        pe.wait_ge(relu_done.sem, relu_done.at(l, h - 3))
                    b = 4 + h % 4
                    nc.tensor.matmul(bank[b][:, 0:P], iq_t[:, h // 4, 0:P], ikz[:, h % 4, 0:P], start=True, stop=True)
                    nc.tensor.matmul(bank[b][:, P:P + T], iq_t[:, h // 4, P:T], ikz[:, h % 4, :], start=True,
                                     stop=True).then_inc(idx_sc.sem, 1)
                pe.wait_ge(relu_done.sem, relu_done.at(l, IDX_HEADS))

                for kind, base in ((0, C_C), (1, C_B)):
                    pe.wait_ge(pn_done.sem, pn_done.at(l, kind + 1))
                    for j in range(4):
                        for t in range(TT):
                            at = (j % 2) * T + t * P
                            last = nc.tensor.transpose(bank[4 + 2 * kind + j // 2][:, at:at + P],
                                                       proj[:, t, base + j * P:base + (j + 1) * P], ident)
                    last.then_inc(pair_tp.sem, 1)

                for g in range(2, 6):
                    gate_slab(l, g)

                pe.wait_ge(gate_out.sem, gate_out.at(l, 6))
                for j in range(3):
                    slab(l, S_UQ + j)
                    token_slab(l, S_UQ + j, 2, 2 * j, Q_RANK, 2, 384, 0, j == 0, j == 2)
                slab(l, S_UKV)
                pe.wait_ge(pq_out.sem, pq_out.at(l, 2))
                pe.wait_ge(kz_out.sem, kz_out.at(l, 4))
                token_slab(l, S_UKV, 2, 6, D, 2, 512, 4, True, True)

                pe.wait_ge(uq_out.sem, uq_out.at(l, 4))
                gate_slab(l, 6)
                pe.wait_ge(ukv_out.sem, ukv_out.at(l, 4))
                for kind, src in ((0, q_a), (1, k_a)):
                    pe.wait_ge(mqk_done.sem, mqk_done.at(l, kind + 1))
                    if kind:
                        gate_slab(l, 7)
                        pe.wait_ge(mla_out_a.sem, mla_out_a.at(l, 2))
                        pe.wait_ge(mla_out_d.sem, mla_out_d.at(l, 2))
                    for h in range(A_HEADS):
                        for t in range(TT):
                            at = (h % 2) * T + t * P
                            m = (t * A_HEADS + h) * A_QK
                            last = nc.tensor.transpose(bank[4 + h // 2][0:A_QK, at:at + P], src[:, m:m + A_QK], ident)
                    last.then_inc(mla_tp.sem, 1)
                pe.wait_ge(mla_out_a.sem, mla_out_a.at(l, 4))
                pe.wait_ge(mla_out_d.sem, mla_out_d.at(l, 4))

                def scores(n):
                    kind, h = HEADS[n]
                    if kind == "a":
                        q, k = qk_t[0:A_QK, h, :], qk_t[0:A_QK, A_HEADS + h, :]
                    else:
                        j = (0 if kind == "c" else 1)
                        q, k = pq_t[:, 2 * j + h // 2, :], kz_t[:, 4 * j + h, :]
                    if n >= 2:
                        pe.wait_ge(ttr_done.sem, ttr_done.at(l, 2 * (n - 1)))
                    b = bank[4 + n % 2]
                    nc.tensor.matmul(b[:, 0:P], q[:, 0:P], k[:, 0:P], start=True, stop=True)
                    nc.tensor.matmul(b[:, P:P + T], q[:, P:T], k[:, :], start=True, stop=True).then_inc(scored.sem, 1)

                def turn_p(n):
                    pe.wait_ge(p_ready.sem, p_ready.at(l, n + 1))
                    if n >= 2:
                        pe.wait_ge(pt_out.sem, pt_out.at(l, n - 1))
                    for j in range(3):
                        last = nc.tensor.transpose(bank[6 + n % 2][:, j * P:(j + 1) * P],
                                                   p_sb[n % 2][:, j * P:(j + 1) * P], ident)
                    last.then_inc(p_tp.sem, 1)

                def weigh_v(n):
                    kind, h = HEADS[n]
                    at = {"a": P * h + A_NOPE, "b": C_BV + HD * h, "c": C_CV + HD * h}[kind]
                    pair = n // 2
                    if n % 2 == 0 and pair >= 2:
                        pe.wait_ge(y_lo_done.sem, y_lo_done.at(l, pair - 1))
                    pe.wait_ge(pt_out.sem, pt_out.at(l, n + 1))
                    r, y = HD * (n % 2), bank[2 + pair % 2]
                    nc.tensor.matmul(y[r:r + HD, 0:T], proj[:, 0, at:at + HD], pt_sb[n % 2][:, 0:T],
                                     start=True, stop=False, skip_group_check=True)
                    nc.tensor.matmul(y[r:r + HD, P:T], proj[:, 1, at:at + HD],
                                     pt_sb[n % 2][:, T:T + P], start=False, stop=True,
                                     skip_group_check=True).then_inc(pv_done.sem, 1)

                scores(0)
                for n in range(NH + 2):
                    if n + 1 < NH:
                        scores(n + 1)
                    if n in GATE_AT:
                        gate_slab(l, 6 + GATE_AT[n])
                    if 1 <= n <= NH:
                        turn_p(n - 1)
                    if n >= 2:
                        weigh_v(n - 2)

                pe.wait_ge(y_lo_done.sem, y_lo_done.at(l, NH // 2))
                pe.wait_ge(gate_out.sem, gate_out.at(l, 12))
                for hf in range(2):
                    banks = ((0, 2, 4), (6, 0, 2))[hf]

                    def branch(b0, s, base, k0, n_k, st):
                        hi, lo = [y_hi[:, k0 + k, :] for k in range(n_k)], [y_lo[:, k0 + k, :] for k in range(n_k)]
                        return channel_slab(s, [(bank[b0 + m // 2][:, (m % 2) * T:(m % 2 + 1) * T], m * P,
                                                 [base + 512 * k for k in range(n_k)], hi, lo, m % 2 == 0)
                                                for m in range(4)], True, True)

                    s = S_BR + 2 * hf
                    slab(l, s)
                    branch(banks[0], s, 0, 0, 4, True).then_inc(slab_used.sem, 1)
                    slab(l, s + 1)
                    if hf:
                        pe.wait_ge(m_done.sem, m_done.at(l, 2))
                    branch(banks[1], s + 1, 0, 4, 2, True)
                    branch(banks[2], s + 1, 1024, 6, 2, True).then_inc(slab_used.sem, 1)

                pe.wait_ge(m_lo.sem, m_lo.at(l, 4))
                for o in range(4):
                    slab(l, S_OUT + o)
                    hi, lo = [h_hi[:, k, :] for k in range(KT)], [h_lo[:, k, :] for k in range(KT)]
                    channel_slab(S_OUT + o, [(bank[4 + o][:, m * T:(m + 1) * T], m * P, [256 * k for k in range(KT)],
                                              hi, lo, m == 0) for m in range(2)], True, True).then_inc(slab_used.sem, 1)

                norm_sums(l, 1, 0)

                def gate_up(s0, step, par, i):
                    pe.wait_ge(glu_done.sem, glu_done.at(l, i - 1))
                    for kg in range(2):
                        slab(l, s0 + kg, step)
                        hi, lo = [h_hi[:, 4 * kg + k, :] for k in range(4)], [h_lo[:, 4 * kg + k, :] for k in range(4)]
                        channel_slab(s0 + kg, [(bank[4 + 2 * par + e][:, m * T:(m + 1) * T], 256 * e + m * P,
                                                [512 * k for k in range(4)], hi, lo, m == 0)
                                               for e in range(2) for m in range(2)],
                                     kg == 0, kg == 1).then_inc(slab_used.sem, 1)

                def down(s0, step, par, i, first=False, final=False):
                    pe.wait_ge(glu_lo_done.sem, glu_lo_done.at(l, i + 1))
                    slab(l, s0, step)
                    hi = [glu_hi[par][:, k * T:(k + 1) * T] for k in range(2)]
                    lo = [glu_lo[par][:, k * T:(k + 1) * T] for k in range(2)]
                    channel_slab(s0, [(bank[m // 2][:, (m % 2) * T:(m % 2 + 1) * T], m * P, [0, D], hi, lo, m % 2 == 0)
                                      for m in range(KT)], first, final).then_inc(slab_used.sem, 1)

                pe.wait_ge(hlo_done.sem, hlo_done.at(l, 8))
                gate_up(S_FF, 0, 0, 1)
                gate_up(S_FF + 2, 0, 1, 1)
                down(S_FF + 4, 0, 0, 0, first=True)
                with pe.Fori(0, FF_PAIRS) as b:
                    for e in range(2):
                        gate_up(S_FFL + 3 * e, 6 * b, e, 2 * b + (e + 2))
                        down(S_FFL + 3 * e + 2, 6 * b, (e + 1) % 2, 2 * b + (e + 1))
                gate_up(S_FFE, 0, 0, FG - 1)
                pe.wait_ge(glu_done.sem, glu_done.at(l, FG - 1))
                mod_columns(l, 2, mod_rows_out.at(l, 4), ada_used.at(l, 2 * KT))
                down(S_FFE + 2, 0, 1, FG - 2)
                down(S_FFE + 3, 0, 0, FG - 1, final=True)

            pe.wait_ge(x_done.sem, x_done.at(DEPTH, 0))
            for t in range(TT):
                for k in range(KT):
                    last = nc.tensor.transpose(bank[2 * t + k // 4][:, (k % 4) * P:(k % 4 + 1) * P],
                                               x_t[:, k, t * P:(t + 1) * P], ident)
                    if k % 4 == 3:
                        last.then_inc(out_tp.sem, 1)

        @block.scalar
        def _(act):
            act.sem_inc(chunk_out.sem, 4)
            act.wait_ge(cols_tp.sem, 1)
            nc.scalar.activation(cols[:, :, :].rearrange("p l r -> p (l r)"), bank[4][:, 0:DEPTH * ROWS],
                                 ACT.Copy).then_inc(cols_ok.sem, 1)
            act.wait_ge(cols_ok.sem, 1)
            nc.scalar.activation(cond[:], cols[:, 0, R_C:R_C + KT], ACT.Silu).then_inc(cond_done.sem, 1)
            for b in range(4):
                act.wait_ge(x_tp.sem, b + 1)
                nc.scalar.activation(x_t[:, 2 * b:2 * b + 2, :].rearrange("p a t -> p (a t)"), bank[b][:, :],
                                     ACT.Copy).then_inc(x_done.sem, 2)

            def mod_rows_copy(l, n):
                act.wait_ge(mod_rows.sem, mod_rows.at(l, n))
                nc.scalar.activation(mod_rows_sb[:, 0:512], bank[6][:, :], ACT.Copy).then_inc(mod_rows_out.sem, 1)
                nc.scalar.activation(mod_rows_sb[0:64, 512:1024], bank[7][0:64, :], ACT.Copy)\
                    .then_inc(mod_rows_out.sem, 1)

            mod_rows_copy(0, 0)

            def hi(l, s0):
                hi_loop(l, s0, 0)

            def hi_loop(l, s0, i):
                slot, n = s0 % RING, slab_words(s0)
                act.wait_ge(raw_in[slot].sem, raw_in[slot].at(l, i * (raw_level(s0 + 6) - raw_level(s0)) + raw_level(s0)))
                act.wait_ge(slab_used.sem, slab_used.at(l, 6 * i + (s0 + 1 - RING)))
                nc.scalar.activation(w_hi[:, slot, 0:n], raw[:, slot, 0:n], ACT.Copy).then_inc(hi_ready.sem, 1)

            def norm(l, which):
                for p in range(4):
                    act.wait_ge(x_done.sem, x_done.at(l, 2 * p + 2 + (8 if which else 0) - 8))
                    nc.scalar.activation(norm_pair(p), x_t[:, 2 * p:2 * p + 2, :].rearrange("p a t -> p (a t)"),
                                         ACT.Square).then_inc(sq_done.sem, 1)
                act.wait_ge(ss_done.sem, ss_done.at(l, which + 1))
                nc.scalar.activation(rstd[:], bank[0 if which else 4][:, 0:T], ACT.Sqrt, bias=eps, scale=1.0 / D)\
                    .then_inc(std_done.sem, 1)
                scale, shift = (mod_b[:, 16:24], mod_b[:, 8:16]) if which else (mod_a[:, 16:24], mod_a[:, 8:16])
                act.wait_ge(coef_done.sem, coef_done.at(l, which + 1))
                for p in range(4):
                    act.wait_ge(hn_done.sem, hn_done.at(l, 4 * which + p + 1))
                    for e in range(2):
                        k = 2 * p + e
                        nc.scalar.activation(h_hi[:, k, :], norm_pair(p)[:, e * T:(e + 1) * T], ACT.Identity,
                                             bias=shift[:, k:k + 1], scale=scale[:, k:k + 1]).then_inc(hhi_done.sem, 1)

            def chunks(l, i, which, loop):
                for cc in which:
                    for j in range(3):
                        s = 3 * cc + j + 2
                        hi_loop(l, s, i) if loop else hi(l, 6 * i + s)
                    act.wait_ge(slab_used.sem, slab_used.at(l, 6 * i + 3 * (cc + 1)))
                    for t in range(TT):
                        nc.scalar.activation(proj[:, t, ds((CHUNKS - 1 - cc) * CW - 2 * CW * i, CW)],
                                             bank[2 * cc + t][:, 0:CW], ACT.Copy).then_inc(chunk_out.sem, 1)

            def gate_act(l, g):
                s = S_GATE0 + g if g < 6 else S_GATE1 + g - 6
                act.wait_ge(slab_used.sem, slab_used.at(l, s + 1))
                nc.scalar.activation(gate(g), bank[gate_bank(g)][:, :], ACT.Tanh, scale=0.5).then_inc(gate_out.sem, 1)

            act.wait_ge(zeros_ok.sem, 3)
            with act.Fori(0, DEPTH) as l:
                link = Chain(act, act_chain, l)
                hi(l, 0)
                hi(l, 1)
                norm(l, 0)
                with act.Fori(0, CHUNKS // 2 - 1) as i:
                    chunks(l, i, (0, 1), True)
                chunks(l, CHUNKS // 2 - 1, (0,), False)
                act.wait_ge(idx_tp.sem, idx_tp.at(l, 1))
                for j in range(2):
                    nc.scalar.activation(iq_t[:, 2 * j:2 * j + 2, :].rearrange("p a t -> p (a t)"), bank[4 + j][:, :],
                                         ACT.Copy).then_inc(iqt_done.sem, 1)
                chunks(l, CHUNKS // 2 - 1, (1,), False)

                mod_rows_copy(l, 1)
                act.wait_ge(chunk_out.sem, chunk_out.at(l, 2 * CHUNKS))
                for m, (c0, n) in enumerate(((0, Q_RANK), (Q_RANK, KV_RANK))):
                    for t in range(TT):
                        if m:
                            act.wait_ge(cq_ss.sem, cq_ss.at(l, t + 1))
                        nc.scalar.activation(acc[:, 1536 + Q_RANK * (t % 2):1536 + Q_RANK * (t % 2) + n],
                                             proj[:, t, c0:c0 + n], ACT.Square,
                                             accum_out=ssc[:, 2 * m + t:2 * m + t + 1]).then_inc(cq_ss.sem, 1)
                act.wait_ge(mod_tp.sem, mod_tp.at(l, 1))

                def pair_squares(kind, base):
                    nc.scalar.activation(acc[:, 0:1024].rearrange("p (t n) -> p t n", t=TT),
                                         proj[:, :, base:base + 512], ACT.Square).then_inc(psq_done.sem, 1)

                pair_squares(0, C_C)
                act.wait_ge(cq_ss.sem, cq_ss.at(l, 4))
                for m, n in ((0, Q_RANK), (1, KV_RANK)):
                    nc.scalar.activation(ssc[:, 2 * m:2 * m + 2], ssc[:, 2 * m:2 * m + 2], ACT.Sqrt, bias=eps,
                                         scale=1.0 / n).then_inc(cq_std.sem, 1)
                hi(l, S_GATE0 + 2)
                act.wait_ge(cq_tp.sem, cq_tp.at(l, 1))
                for k in range(KT):
                    nc.scalar.activation(y_hi[:, k, :], bank[k // 2][:, (k % 2) * T:(k % 2 + 1) * T], ACT.Copy,
                                         scale=pcol[:, R_GQ + k:R_GQ + k + 1]).then_inc(cq_hi.sem, 1)
                act.wait_ge(pss_done.sem, pss_done.at(l, 1))
                pair_squares(1, C_B)
                for kind, ss in ((0, ss16), (1, ss16b)):
                    act.wait_ge(pss_done.sem, pss_done.at(l, kind + 1))
                    nc.scalar.activation(ss, ss, ACT.Sqrt, bias=eps, scale=1.0 / HD).then_inc(pstd_done.sem, 1)
                gate_act(l, 0)
                hi(l, S_GATE0 + 3)
                gate_act(l, 1)
                hi(l, S_GATE0 + 4)
                for h in range(IDX_HEADS):
                    act.wait_ge(idx_sc.sem, idx_sc.at(l, h + 1))
                    if h >= 4:
                        act.wait_ge(idx_acc.sem, idx_acc.at(l, 2 * (h - 3)))
                    nc.scalar.activation(relu_b[h % 4], bank[4 + h % 4][:, 0:P + T], ACT.Relu).then_inc(relu_done.sem, 1)
                for kind in range(2):
                    act.wait_ge(pair_tp.sem, pair_tp.at(l, kind + 1))
                    nc.scalar.activation(pq_t[:, 2 * kind:2 * kind + 2, :].rearrange("p a t -> p (a t)"),
                                         bank[4 + 2 * kind][:, :], ACT.Copy).then_inc(pq_out.sem, 1)
                act.wait_ge(kr_done.sem, kr_done.at(l, 1))
                for g in range(2, 6):
                    gate_act(l, g)
                    hi(l, S_GATE0 + g + 3)
                for j in range(2):
                    hi(l, S_UQ + 3 + j)

                act.wait_ge(cq_rstd.sem, cq_rstd.at(l, 1))
                act.wait_ge(slab_used.sem, slab_used.at(l, S_UQ + 3))
                for t in range(TT):
                    for ch in range(2):
                        at = t * Q_RANK + 384 * ch
                        nc.scalar.activation(q_a[:, at:at + 384], bank[2 * t + ch][:, 0:384], ACT.Copy,
                                             scale=ssc[:, t:t + 1]).then_inc(uq_out.sem, 1)
                act.wait_ge(uq_out.sem, uq_out.at(l, 4))
                nc.scalar.activation(sq, q_a, ACT.Square).then_inc(msq_done.sem, 1)
                hi(l, S_UKV + 2)
                act.wait_ge(slab_used.sem, slab_used.at(l, S_UKV + 1))
                for t in range(TT):
                    for ch in range(2):
                        nc.scalar.activation(proj[:, t, 512 * ch:512 * (ch + 1)], bank[4 + 2 * t + ch][:, :], ACT.Copy,
                                             scale=ssc[:, 2 + t:3 + t]).then_inc(ukv_out.sem, 1)
                act.wait_ge(ukv_out.sem, ukv_out.at(l, 4))
                act.wait_ge(mss_done.sem, mss_done.at(l, 1))
                nc.scalar.activation(acc[:, 0:1024].rearrange("p (t h d) -> p t h d", t=TT, h=A_HEADS), k_nope,
                                     ACT.Square).then_inc(msq_done.sem, 1)
                for kind, ss in ((0, ss16), (1, ss16b)):
                    act.wait_ge(mss_done.sem, mss_done.at(l, kind + 1))
                    nc.scalar.activation(ss, ss, ACT.Sqrt, bias=eps, scale=1.0 / A_QK).then_inc(mstd_done.sem, 1)
                hi(l, S_GATE1 + 2)
                for kind in range(2):
                    act.wait_ge(mla_tp.sem, mla_tp.at(l, kind + 1))
                    for b in range(2):
                        m = A_HEADS * kind + 2 * b
                        nc.scalar.activation(qk_t[0:A_QK, m:m + 2, :].rearrange("p a t -> p (a t)"),
                                             bank[4 + b][0:A_QK, :], ACT.Copy).then_inc(mla_out_a.sem, 1)
                    if kind == 0:
                        hi(l, S_GATE1 + 3)
                gate_act(l, 6)
                gate_act(l, 7)

                def expo(n):
                    kind, h = HEADS[n]
                    slope = head_slope(kind, h)
                    act.wait_ge(maxed.sem, maxed.at(l, n + 1))
                    for t, (c0, c1) in enumerate(((0, P), (P, P + T))):
                        nc.scalar.activation(p_sb[n % 2][:, c0:c1], p_sb[n % 2][:, c0:c1], ACT.Exp,
                                             bias=negmax[n % 2][:, t:t + 1], scale=slope,
                                             accum_out=rowsum[n % 2][:, t:t + 1]).then_inc(exped.sem, 1)

                for n in range(NH + 2):
                    if n < NH:
                        expo(n)
                    if 1 <= n <= NH:
                        act.wait_ge(p_tp.sem, p_tp.at(l, n))
                        if n >= 3:
                            act.wait_ge(pv_done.sem, pv_done.at(l, n - 2))
                        nc.scalar.activation(pt_sb[(n - 1) % 2], bank[6 + (n - 1) % 2][:, 0:P + T], ACT.Copy)\
                            .then_inc(pt_out.sem, 1)
                    if n >= 3 and n % 2:
                        pair = (n - 3) // 2
                        act.wait_ge(pv_done.sem, pv_done.at(l, 2 * pair + 2))
                        nc.scalar.activation(y_hi[:, PAIR_Y[pair], :], bank[2 + pair % 2][:, 0:T],
                                             ACT.Copy).then_inc(y_hi_done.sem, 1)
                    if n - 1 in GATE_AT:
                        hi(l, S_GATE1 + 2 + GATE_AT[n - 1])
                        gate_act(l, 6 + GATE_AT[n - 1])

                for hf in range(2):
                    for m in range(2):
                        hi(l, S_BR + 2 + 2 * hf + m)
                    for q in range(2):
                        act.wait_ge(m_done.sem, m_done.at(l, 2 * hf + q + 1))
                        k = 4 * hf + 2 * q
                        nc.scalar.activation(h_hi[:, k:k + 2, :].rearrange("p a t -> p (a t)"),
                                             merged(hf)[:, 512 * q:512 * (q + 1)], ACT.Copy, scale=0.5)\
                            .then_inc(m_hi.sem, 1)
                for s in range(S_OUT + 2, S_FF + 2):
                    hi(l, s)
                norm(l, 1)

                def silu_glu(s_last, step, par, i):
                    act.wait_ge(slab_used.sem, slab_used.at(l, step + (s_last + 1)))
                    nc.scalar.activation(silu_g[par], bank[4 + 2 * par][:, :], ACT.Silu).then_inc(silu_done.sem, 1)
                    act.wait_ge(glu_done.sem, glu_done.at(l, i + 1))
                    nc.scalar.activation(glu_hi[par], glu[par], ACT.Copy).then_inc(glu_hi_done.sem, 1)

                hi(l, S_FF + 2)
                silu_glu(S_FF + 1, 0, 0, 0)
                hi(l, S_FF + 3)
                hi(l, S_FF + 4)
                hi(l, S_FF + 5)
                silu_glu(S_FF + 3, 0, 1, 1)
                hi(l, S_FF + 6)
                with act.Fori(0, FF_PAIRS) as b:
                    for e in range(2):
                        hi_loop(l, S_FFL + 3 * e + 2, b)
                        hi_loop(l, S_FFL + 3 * e + 3, b)
                        silu_glu(S_FFL + 3 * e + 1, 6 * b, e, 2 * b + (e + 2))
                        hi_loop(l, S_FFL + 3 * e + 4, b)
                hi(l, S_FFE + 2)
                hi(l, S_FFE + 3)
                silu_glu(S_FFE + 1, 0, 0, FG - 1)
                mod_rows_copy(l, 2)

            for b in range(4):
                act.wait_ge(out_tp.sem, b + 1)
                nc.scalar.activation(proj[:, b // 2, (b % 2) * 512:(b % 2 + 1) * 512], bank[b][:, :], ACT.Copy)\
                    .then_inc(out_rows.sem, 1)

        @block.vector
        def _(dve):
            dve.sem_inc(lo_ready.sem, RING)
            dve.sem_inc(glu_done.sem, 1)
            dve.wait_ge(cond_done.sem, 1)
            dve.wait_ge(acc_zero.sem, 1)
            for k in range(KT):
                dve.wait_ge(apro_in[k % 3].sem, 16 * (k // 3 + 1))
                if k:
                    dve.wait_ge(ada_used.sem, k)
                nc.vector.scalar_tensor_tensor(out=acc[:, D:3 * D], in0=ada_pro[k % 3], scalar=cond[:, k:k + 1],
                                               in1=acc[:, D:3 * D], op0=ALU.mult, op1=ALU.add)\
                    .then_inc(ada_used.sem, 1)

            def mod_get(l, n, mod):
                dve.wait_ge(mod_tp.sem, mod_tp.at(l, n))
                v0 = bank[6][:, :].rearrange("p (b j r) -> p j b r", b=4, j=4, r=32)[:, :, :, 0]
                v1 = bank[7][:, 0:256].rearrange("p (b j r) -> p j b r", b=4, j=2, r=32)[:, :, :, 0]
                link(nc.vector.tensor_copy(mod[:, 0:16].rearrange("p (j b) -> p j b", j=4), v0))
                nc.vector.tensor_copy(mod[:, 16:24].rearrange("p (j b) -> p j b", j=2), v1).then_inc(mod_got.sem, 1)
                dve.wait_ge(mod_got.sem, mod_got.at(l, n))

            link = Chain(dve, dve_pro, 0)
            mod_get(0, 0, mod_a)

            def lo(l, s0, i=0):
                slot, n = s0 % RING, slab_words(s0)
                dve.wait_ge(hi_ready.sem, hi_ready.at(l, 6 * i + (s0 + 1)))
                nc.vector.tensor_tensor(w_lo[:, slot, 0:n], raw[:, slot, 0:n], w_hi[:, slot, 0:n], ALU.subtract)\
                    .then_inc(lo_ready.sem, 1)

            def coefficients(l, which, mod, c0, gain_row):
                link(nc.vector.scalar_tensor_tensor(out=mod[:, 16:24], in0=mod[:, 16:24], scalar=1.0,
                                                    in1=pcol[:, gain_row:gain_row + 8], op0=ALU.add, op1=ALU.mult))
                dve.sem_inc(coef_done.sem, 1)

            def norm(l, which):
                dve.wait_ge(std_done.sem, std_done.at(l, which + 1))
                link(nc.vector.reciprocal(rstd[:], rstd[:]))
                scale, shift = (mod_b[:, 16:24], mod_b[:, 8:16]) if which else (mod_a[:, 16:24], mod_a[:, 8:16])
                for p in range(4):
                    nc.vector.tensor_tensor(norm_pair(p).rearrange("p (a t) -> p a t", a=2), x_t[:, 2 * p:2 * p + 2, :],
                                            rstd[:].unsqueeze(1).to_broadcast([P, 2, T]), ALU.mult)\
                        .then_inc(hn_done.sem, 1)
                for p in range(4):
                    dve.wait_ge(hhi_done.sem, hhi_done.at(l, 8 * which + 2 * p + 2))
                    for e in range(2):
                        k = 2 * p + e
                        v = norm_pair(p)[:, e * T:(e + 1) * T]
                        ins = nc.vector.tensor_scalar(v, v, scale[:, k:k + 1], shift[:, k:k + 1], ALU.mult, ALU.add)
                        link(ins)
                    nc.vector.tensor_tensor(h_lo[:, 2 * p:2 * p + 2, :].rearrange("p a t -> p (a t)"), norm_pair(p),
                                            h_hi[:, 2 * p:2 * p + 2, :].rearrange("p a t -> p (a t)"), ALU.subtract)\
                        .then_inc(hlo_done.sem, 1)

            def pick_cond(l, i, n, before):
                dve.wait_ge(ada_used.sem, ada_used.at(l, before))
                nc.vector.tensor_copy(cond_now[:], cond[:, ds(2 * i, 2)]).then_inc(cond_ok.sem, 1)
                dve.wait_ge(cond_ok.sem, cond_ok.at(l, n))

            def ada_step(l, m, landed, e):
                dve.wait_ge(ada_in[e].sem, landed)
                dve.wait_ge(ada_used.sem, ada_used.at(l, m))
                nc.vector.scalar_tensor_tensor(out=acc[:], in0=ada_raw[e], scalar=cond_now[:, e:e + 1], in1=acc[:],
                                               op0=ALU.mult, op1=ALU.add).then_inc(ada_used.sem, 1)

            def chunk(l, i, cc):
                for j in range(3):
                    lo(l, 3 * cc + j + 2, i) if not isinstance(i, int) else lo(l, 6 * i + 3 * cc + j + 2)
                ada_step(l, 2 * i + cc, ada_in[cc].at(l, 16 * i + 16), cc)

            with dve.Fori(0, DEPTH) as l:
                link = Chain(dve, dve_chain, l)
                link(nc.vector.tensor_copy(pcol[:].unsqueeze(1), cols[:, ds(l, 1), :]))
                link(nc.vector.tensor_tensor(mod_a[:, 8:24], mod_a[:, 8:24], pcol[:, 0:16], ALU.add))
                coefficients(l, 0, mod_a, 0, R_N1)
                lo(l, 0)
                lo(l, 1)
                norm(l, 0)
                dve.wait_ge(acc_zero.sem, acc_zero.at(l, 1))
                apart(dve)
                with dve.Fori(0, CHUNKS // 2 - 1) as i:
                    pick_cond(l, i, i + 1, 2 * i)
                    chunk(l, i, 0)
                    chunk(l, i, 1)
                last = CHUNKS // 2 - 1
                pick_cond(l, last, last + 1, 2 * last)
                chunk(l, last, 0)
                dve.wait_ge(chunk_out.sem, chunk_out.at(l, 12))
                for t in range(TT):
                    nc.vector.tensor_copy(ik_rep[:, t, :].rearrange("p (r d) -> p r d", r=4),
                                          proj[:, t, C_IK:C_IK + IDX_DIM].unsqueeze(1).to_broadcast([P, 4, IDX_DIM]))\
                        .then_inc(ikrep_done.sem, 1)
                dve.wait_ge(idx_tp.sem, idx_tp.at(l, 1))
                for r in range(4):
                    q = slice(32 * r, 32 * r + 32)
                    nc.vector.tensor_copy(ikz[q, r, :], bank[6][q, 0:T]).then_inc(ikz_done.sem, 1)
                chunk(l, last, 1)

                lo(l, S_GATE0 + 2)
                mod_get(l, 1, mod_b)
                link(nc.vector.tensor_tensor(mod_b[:], mod_b[:], pcol[:, 16:40], ALU.add))
                coefficients(l, 1, mod_b, 0, R_N2)

                def pair_sums(kind, ss):
                    dve.wait_ge(psq_done.sem, psq_done.at(l, kind + 1))
                    nc.vector.tensor_reduce(ss, acc[:, 0:1024].rearrange("p (m d) -> p m d", d=HD), AX_X, ALU.add)\
                        .then_inc(pss_done.sem, 1)

                pair_sums(0, ss16)
                dve.wait_ge(cq_std.sem, cq_std.at(l, 2))
                nc.vector.reciprocal(ssc, ssc).then_inc(cq_rstd.sem, 1)
                for k in range(KT):
                    dve.wait_ge(cq_hi.sem, cq_hi.at(l, 2 * (k // 2) + 2))
                    nc.vector.scalar_tensor_tensor(out=y_lo[:, k, :], in0=bank[k // 2][:, (k % 2) * T:(k % 2 + 1) * T],
                                                   scalar=pcol[:, R_GQ + k:R_GQ + k + 1], in1=y_hi[:, k, :],
                                                   op0=ALU.mult, op1=ALU.subtract).then_inc(cq_lo.sem, 1)
                pair_sums(1, ss16b)

                dve.wait_ge(gains_in.sem, gains_in.at(l, 16 * 6))
                kr = proj[:, :, C_KR:C_KR + A_ROPE]
                half = A_ROPE // 2
                cos = konst[:, K_COS:K_COS + TT * A_ROPE].rearrange("p (t d) -> p t d", t=TT)
                sin = konst[:, K_SIN:K_SIN + TT * A_ROPE].rearrange("p (t d) -> p t d", t=TT)
                link(nc.vector.tensor_tensor(krw[:], kr, kr, ALU.mult))
                link(nc.vector.tensor_reduce(krss, krw[:], AX_X, ALU.add))
                link(nc.vector.tensor_tensor(kr, kr, gains[:, A_QK + A_NOPE:2 * A_QK].unsqueeze(1)
                                             .to_broadcast([P, TT, A_ROPE]), ALU.mult))
                nc.vector.tensor_tensor(krr[:], kr, cos, ALU.mult)
                nc.vector.tensor_tensor(krw[:, :, 0:half], kr[:, :, half:], sin[:, :, 0:half], ALU.mult)
                link(nc.vector.tensor_tensor(krw[:, :, half:], kr[:, :, 0:half], sin[:, :, half:], ALU.mult))
                link(nc.vector.tensor_tensor(krr[:], krr[:], krw[:], ALU.add))
                dve.sem_inc(kr_done.sem, 1)

                def pair_norm(kind, base, ss, g0, fac):
                    dve.wait_ge(pstd_done.sem, pstd_done.at(l, kind + 1))
                    v = proj[:, :, base:base + 512].rearrange("p t (g d) -> p t g d", d=HD)
                    link(nc.vector.reciprocal(ss, ss))
                    link(nc.vector.tensor_tensor(ss, ss, konst[:, fac:fac + 16], ALU.mult))
                    for m in range(2):
                        gm = gains[:, g0 + HD * m:g0 + HD * (m + 1)].unsqueeze(1).unsqueeze(1)\
                            .to_broadcast([P, TT, 4, HD])
                        ins = nc.vector.tensor_tensor(v[:, :, 4 * m:4 * m + 4, :], v[:, :, 4 * m:4 * m + 4, :], gm,
                                                      ALU.mult)
                    link(ins)
                    nc.vector.tensor_tensor(v, v, ss.rearrange("p (t g) -> p t g", t=TT).unsqueeze(3)
                                            .to_broadcast([P, TT, 8, HD]), ALU.mult).then_inc(pn_done.sem, 1)

                pair_norm(0, C_C, ss16, 2 * A_QK + 2 * HD, K_FAC + 16)
                lo(l, S_GATE0 + 3)
                pair_norm(1, C_B, ss16b, 2 * A_QK, K_FAC)

                for h in range(IDX_HEADS):
                    dve.wait_ge(relu_done.sem, relu_done.at(l, h + 1))
                    if h:
                        dve.wait_ge(idx_acc.sem, idx_acc.at(l, 2 * h))
                    for t, (c0, c1) in enumerate(((0, P), (P, P + T))):
                        wt = proj[:, t, C_IW + h:C_IW + h + 1]
                        if h == 0:
                            ins = nc.vector.tensor_scalar(score[:, c0:c1], relu_b[h % 4][:, c0:c1], wt, None, ALU.mult)
                        else:
                            ins = nc.vector.scalar_tensor_tensor(out=score[:, c0:c1], in0=relu_b[h % 4][:, c0:c1],
                                                                 scalar=wt, in1=score[:, c0:c1], op0=ALU.mult,
                                                                 op1=ALU.add)
                        ins.then_inc(idx_acc.sem, 1)
                    if h == 7:
                        lo(l, S_GATE0 + 4)
                dve.wait_ge(idx_acc.sem, idx_acc.at(l, 2 * IDX_HEADS))
                link(nc.vector.scalar_tensor_tensor(out=score[:], in0=score[:], scalar=IDX_SCALE, in1=causal,
                                                    op0=ALU.mult, op1=ALU.add))

                def top_keys(t, rounds):
                    v = score[:, 0:P] if t == 0 else score[:, P:P + T]
                    for _ in range(rounds):
                        apart(dve)
                        link(nc.vector.max(top8, v))
                        apart(dve)
                        link(nc.vector.match_replace(v, top8, v, TAKEN))

                def k_rows(kind):
                    dve.wait_ge(pair_tp.sem, pair_tp.at(l, kind + 1))
                    for e in range(2):
                        q = slice(HD * e, HD * (e + 1))
                        nc.vector.tensor_copy(kz_t[q, 4 * kind + e:4 * kind + 4:2, :],
                                              bank[5 + 2 * kind][q, :].rearrange("p (a t) -> p a t", a=2))\
                            .then_inc(kz_out.sem, 1)

                k_rows(0)
                k_rows(1)
                top_keys(0, 4)
                lo(l, S_GATE0 + 5)
                top_keys(0, 4)
                lo(l, S_UQ)
                top_keys(1, 3)
                lo(l, S_UQ + 1)
                top_keys(1, 3)
                lo(l, S_UQ + 2)
                top_keys(1, 2)
                link(nc.vector.tensor_scalar(score[:], score[:], TAKEN / 2, NEG, ALU.is_ge, ALU.mult))
                nc.vector.tensor_tensor(sel_nd[:], score[:], neg_dist, ALU.add).then_inc(nd_done.sem, 1)
                lo(l, S_UKV)
                lo(l, S_GATE1)

                dve.wait_ge(msq_done.sem, msq_done.at(l, 1))
                nc.vector.tensor_reduce(ss16, sq.rearrange("p (m d) -> p m d", d=A_QK), AX_X, ALU.add)\
                    .then_inc(mss_done.sem, 1)
                qv = q_a.rearrange("p (m d) -> p m d", d=A_QK)
                q4 = q_a.rearrange("p (t h d) -> p t h d", t=TT, h=A_HEADS)
                link(nc.vector.tensor_tensor(qv, qv, gains[:, 0:A_QK].unsqueeze(1).to_broadcast([P, 16, A_QK]), ALU.mult))
                lo(l, S_GATE1 + 1)
                rot = q4[:, :, :, A_NOPE:A_QK]
                ra = acc[:, 1536:2048].rearrange("p (t h d) -> p t h d", t=TT, h=A_HEADS)
                rb = acc[:, 2048:2560].rearrange("p (t h d) -> p t h d", t=TT, h=A_HEADS)
                nc.vector.tensor_tensor(ra, rot, cos.unsqueeze(2).to_broadcast([P, TT, A_HEADS, A_ROPE]), ALU.mult)
                nc.vector.tensor_tensor(rb[:, :, :, 0:half], rot[:, :, :, half:], sin[:, :, 0:half].unsqueeze(2)
                                        .to_broadcast([P, TT, A_HEADS, half]), ALU.mult)
                link(nc.vector.tensor_tensor(rb[:, :, :, half:], rot[:, :, :, 0:half], sin[:, :, half:].unsqueeze(2)
                                             .to_broadcast([P, TT, A_HEADS, half]), ALU.mult))
                link(nc.vector.tensor_tensor(rot, ra, rb, ALU.add))
                dve.wait_ge(msq_done.sem, msq_done.at(l, 2))
                link(nc.vector.tensor_reduce(ss16b, acc[:, 0:1024].rearrange("p (m d) -> p m d", d=A_NOPE), AX_X,
                                             ALU.add))
                sb3 = ss16b.rearrange("p (t h) -> p t h", t=TT)
                nc.vector.tensor_tensor(sb3, sb3, krss.unsqueeze(2).to_broadcast([P, TT, A_HEADS]), ALU.add)\
                    .then_inc(mss_done.sem, 1)
                dve.wait_ge(mstd_done.sem, mstd_done.at(l, 1))
                link(nc.vector.reciprocal(ss16, ss16))
                link(nc.vector.tensor_scalar(ss16, ss16, float(A_QK ** -0.5), None, ALU.mult))
                nc.vector.tensor_tensor(qv, qv, ss16.unsqueeze(2).to_broadcast([P, 16, A_QK]), ALU.mult)\
                    .then_inc(mqk_done.sem, 1)
                kv = k_a.rearrange("p (t h d) -> p t h d", t=TT, h=A_HEADS)
                link(nc.vector.tensor_tensor(kv[:, :, :, 0:A_NOPE], k_nope, gains[:, A_QK:A_QK + A_NOPE].unsqueeze(1)
                                             .unsqueeze(1).to_broadcast([P, TT, A_HEADS, A_NOPE]), ALU.mult))
                dve.wait_ge(mstd_done.sem, mstd_done.at(l, 2))
                link(nc.vector.reciprocal(ss16b, ss16b))
                nc.vector.tensor_tensor(kv[:, :, :, 0:A_NOPE], kv[:, :, :, 0:A_NOPE],
                                        sb3.unsqueeze(3).to_broadcast([P, TT, A_HEADS, A_NOPE]), ALU.mult)
                nc.vector.tensor_tensor(kv[:, :, :, A_NOPE:], krr[:].unsqueeze(2).to_broadcast([P, TT, A_HEADS, A_ROPE]),
                                        sb3.unsqueeze(3).to_broadcast([P, TT, A_HEADS, A_ROPE]), ALU.mult)\
                    .then_inc(mqk_done.sem, 1)
                lo(l, S_GATE1 + 2)
                for kind in range(2):
                    dve.wait_ge(mla_tp.sem, mla_tp.at(l, kind + 1))
                    for b in range(2, 4):
                        m = A_HEADS * kind + 2 * b
                        nc.vector.tensor_copy(qk_t[0:A_QK, m:m + 2, :].rearrange("p a t -> p (a t)"),
                                              bank[4 + b][0:A_QK, :]).then_inc(mla_out_d.sem, 1)
                    if kind == 0:
                        lo(l, S_GATE1 + 3)
                dve.wait_ge(nd_done.sem, nd_done.at(l, 1))

                def scores_max(n):
                    kind, h = HEADS[n]
                    mask = {"a": causal, "b": neg_dist, "c": sel_nd[:]}[kind]
                    slope = head_slope(kind, h)
                    dve.wait_ge(scored.sem, scored.at(l, n + 1))
                    if n >= 2:
                        dve.wait_ge(p_tp.sem, p_tp.at(l, n - 1))
                    apart(dve)
                    for t, (c0, c1) in enumerate(((0, P), (P, P + T))):
                        nc.vector.tensor_tensor_reduce(p_sb[n % 2][:, c0:c1], bank[4 + n % 2][:, c0:c1], mask[:, c0:c1],
                                                       1.0, NEG, ALU.add, ALU.max, rowmax[n % 2][:, t:t + 1])\
                            .then_inc(ttr_done.sem, 1)
                    dve.wait_ge(ttr_done.sem, ttr_done.at(l, 2 * n + 2))
                    nc.vector.tensor_scalar(negmax[n % 2], rowmax[n % 2], -slope, None, ALU.mult)\
                        .then_inc(maxed.sem, 1)

                def normalize(n):
                    dve.wait_ge(exped.sem, exped.at(l, 2 * n + 2))
                    link(nc.vector.reciprocal(rinv[n % 2], rowsum[n % 2]))
                    for t, (c0, c1) in enumerate(((0, P), (P, P + T))):
                        ins = nc.vector.tensor_scalar(p_sb[n % 2][:, c0:c1], p_sb[n % 2][:, c0:c1],
                                                      rinv[n % 2][:, t:t + 1], None, ALU.mult)
                    ins.then_inc(p_ready.sem, 1)

                for n in range(NH + 2):
                    if n < NH:
                        scores_max(n)
                    if 1 <= n <= NH:
                        normalize(n - 1)
                    if n >= 3 and n % 2:
                        pair = (n - 3) // 2
                        dve.wait_ge(y_hi_done.sem, y_hi_done.at(l, pair + 1))
                        nc.vector.tensor_tensor(y_lo[:, PAIR_Y[pair], :], bank[2 + pair % 2][:, 0:T],
                                                y_hi[:, PAIR_Y[pair], :], ALU.subtract).then_inc(y_lo_done.sem, 1)
                    if n - 1 in GATE_AT:
                        lo(l, S_GATE1 + 2 + GATE_AT[n - 1])

                for hf in range(2):
                    banks = ((0, 2, 4), (6, 0, 2))[hf]
                    for m in range(2):
                        lo(l, S_BR + 2 + 2 * hf + m)
                    dve.wait_ge(slab_used.sem, slab_used.at(l, S_BR + 2 * hf + 2))
                    for q in range(2):
                        g = 2 * hf + q
                        m_ = merged(hf)[:, 512 * q:512 * (q + 1)]
                        dst = [m_, gate(4 + g), gate(8 + g)]
                        for br in range(3):
                            ins = nc.vector.scalar_tensor_tensor(out=dst[br], in0=gate(4 * br + g), scalar=1.0,
                                                                 in1=bank[banks[br] + q][:, :], op0=ALU.add,
                                                                 op1=ALU.mult)
                        link(ins)
                        link(nc.vector.tensor_tensor(m_, m_, dst[1], ALU.add))
                        nc.vector.tensor_tensor(m_, m_, dst[2], ALU.add).then_inc(m_done.sem, 1)
                    for q in range(2):
                        k = 4 * hf + 2 * q
                        dve.wait_ge(m_hi.sem, m_hi.at(l, 2 * hf + q + 1))
                        nc.vector.scalar_tensor_tensor(out=h_lo[:, k:k + 2, :].rearrange("p a t -> p (a t)"),
                                                       in0=merged(hf)[:, 512 * q:512 * (q + 1)], scalar=0.5,
                                                       in1=h_hi[:, k:k + 2, :].rearrange("p a t -> p (a t)"),
                                                       op0=ALU.mult, op1=ALU.subtract).then_inc(m_lo.sem, 1)
                for o in range(4):
                    lo(l, S_OUT + o + 2)
                    dve.wait_ge(slab_used.sem, slab_used.at(l, S_OUT + o + 1))
                    for e in range(2):
                        k = 2 * o + e
                        nc.vector.scalar_tensor_tensor(out=x_t[:, k, :], in0=bank[4 + o][:, e * T:(e + 1) * T],
                                                       scalar=mod_b[:, k:k + 1], in1=x_t[:, k, :], op0=ALU.mult,
                                                       op1=ALU.add).then_inc(x_done.sem, 1)
                norm(l, 1)

                def glu_step(par, i):
                    dve.wait_ge(silu_done.sem, silu_done.at(l, i + 1))
                    nc.vector.tensor_tensor(glu[par], silu_g[par], bank[5 + 2 * par][:, :], ALU.mult)\
                        .then_inc(glu_done.sem, 1)
                    dve.wait_ge(glu_hi_done.sem, glu_hi_done.at(l, i + 1))
                    nc.vector.tensor_tensor(glu_lo[par], glu[par], glu_hi[par], ALU.subtract)\
                        .then_inc(glu_lo_done.sem, 1)

                lo(l, S_FF + 2)
                glu_step(0, 0)
                lo(l, S_FF + 3)
                lo(l, S_FF + 4)
                lo(l, S_FF + 5)
                glu_step(1, 1)
                lo(l, S_FF + 6)
                dve.wait_ge(acc_zero.sem, acc_zero.at(l, 2))
                apart(dve)
                with dve.Fori(0, FF_PAIRS) as b:
                    pick_cond(l, b, b + 5, 2 * b + KT)
                    for e in range(2):
                        lo(l, S_FFL + 3 * e + 2, b)
                        lo(l, S_FFL + 3 * e + 3, b)
                        glu_step(e, 2 * b + (e + 2))
                        lo(l, S_FFL + 3 * e + 4, b)
                        m = 2 * b + (e + KT)
                        ada_step(l, m, ada_in[e].at(l, 32 * (b + 1) + 16 * (KT // 2)), e)
                lo(l, S_FFE + 2)
                lo(l, S_FFE + 3)
                glu_step(0, FG - 1)
                mod_get(l, 2, mod_a)
                link(nc.vector.tensor_tensor(mod_a[:, 0:8], mod_a[:, 0:8], pcol[:, 40:48], ALU.add))
                dve.wait_ge(slab_used.sem, slab_used.at(l, NS))
                for k in range(KT):
                    nc.vector.scalar_tensor_tensor(out=x_t[:, k, :], in0=bank[k // 2][:, (k % 2) * T:(k % 2 + 1) * T],
                                                   scalar=mod_a[:, k:k + 1], in1=x_t[:, k, :], op0=ALU.mult,
                                                   op1=ALU.add).then_inc(x_done.sem, 1)
                assert link.n == DVE_LINKS, link.n


_INS = ["x", "c", "w_ada", "b_ada", "norm1", "w_in", "g_cq", "w_uq", "g_ckv", "w_ukv", "qn_mla", "kn_mla", "qn_moba",
        "kn_moba", "qn_dsa", "kn_dsa", "w_br_a", "w_br_b", "w_br_c", "w_out", "norm2", "w_gu", "w_down"]


def kernel(**inputs):
    import concourse.bacc as bacc
    from concourse.bass_utils import run_bass_kernel_spmd

    nc = bacc.Bacc("TRN2", target_bir_lowering=False, num_devices=1)
    arrays = {f"in_{n}_dram": np.ascontiguousarray(inputs[n]) for n in _INS}
    arrays["in_const_dram"] = constants()
    args = [nc.dram_tensor(n, a.shape, mybir.dt.from_np(a.dtype), kind="ExternalInput").ap() for n, a in arrays.items()]
    out = nc.dram_tensor("out_0_dram", (1, T, D), F32, kind="ExternalOutput").ap()
    build(nc, *args, out)
    r = run_bass_kernel_spmd(nc, [arrays], core_ids=[0])
    return r.results[0]["out_0_dram"]
```

```python
from contextlib import ExitStack

import numpy as np

import concourse.bass as bass
from concourse import mybir
from concourse.bass import ds

F32 = mybir.dt.float32
F32R = mybir.dt.float32r
ALU = mybir.AluOpType
ACT = mybir.ActivationFunctionType
AX_X = mybir.AxisListType.X

P = 128
D = 1024
T = 256
DEPTH = 2
KT = D // P
TT = T // P
HD = 64
EPS = 1e-6
ROPE_THETA = 10000.0

A_HEADS, A_NOPE, A_ROPE, A_QK, A_V = 8, 64, 32, 96, 64
Q_RANK, KV_RANK = 768, 256
B_HEADS = C_HEADS = 4
IDX_HEADS, IDX_DIM = 16, 32
N_KEEP = min(256, T // 4)
D_FF = -(-8 * D // (3 * 256)) * 256

C_CKV = Q_RANK
C_KR = C_CKV + KV_RANK
C_B = C_KR + A_ROPE
C_C = C_B + 3 * B_HEADS * HD
C_IQ = C_C + 3 * C_HEADS * HD
C_IK = C_IQ + IDX_HEADS * IDX_DIM
C_IW = C_IK + IDX_DIM
C_G = C_IW + IDX_HEADS
C_BV = C_B + 2 * B_HEADS * HD
C_CV = C_C + 2 * C_HEADS * HD

RING = 3
SLAB = 2048
CHUNKS = 8
CW = C_G // CHUNKS
KGRP = [(0, 3), (3, 3), (6, 2)]
S_GATE0 = CHUNKS * len(KGRP)
S_UQ = S_GATE0 + 2
S_UKV = S_UQ + 3
S_GATE1 = S_UKV + 1
S_BR = S_GATE1 + 10
S_OUT = S_BR + 4
S_FF = S_OUT + 4
FG = D_FF // 256
NS = S_FF + 3 * FG
S_FFL = S_FF + 5
FF_PAIRS = (FG - 3) // 2
S_FFE = S_FFL + 6 * FF_PAIRS
NEG = -1.0e30
TAKEN = -3.0e38
IDX_SCALE = float((IDX_DIM * IDX_HEADS) ** -0.5)
SLOPES = [2.0 ** (-8.0 * (i + 1) / (B_HEADS + C_HEADS)) for i in range(B_HEADS + C_HEADS)]
ADA_T0, ADA_TN = 2 * D, 3 * D
ROWS = 48 + 8 + 8 + 6 + 2 + 8
R_N1, R_N2, R_GQ, R_GKV, R_C = 48, 56, 64, 70, 72

K_ID = 0
K_CM = K_ID + P
K_ND = K_CM + P + T
K_COS = K_ND + P + T
K_SIN = K_COS + TT * A_ROPE
K_FAC = K_SIN + TT * A_ROPE
K_ALL = K_FAC + 2 * TT * 2 * B_HEADS


def constants():
    t = np.zeros((P, K_ALL), np.float32)
    t[:, K_ID:K_ID + P] = np.eye(P)
    for tok in range(TT):
        q = tok * P + np.arange(P)[:, None]
        k = np.arange(P * (tok + 1))[None, :]
        at = tok * P
        t[:, K_CM + at:K_CM + at + k.size] = np.where(k <= q, 0.0, NEG)
        t[:, K_ND + at:K_ND + at + k.size] = np.where(k <= q, -(q - k), NEG)
        half = A_ROPE // 2
        freqs = np.float32(ROPE_THETA) ** (-np.arange(half, dtype=np.float32) / np.float32(half))
        ang = q.astype(np.float32) * freqs[None, :].astype(np.float32)
        cos, sin = np.cos(ang), np.sin(ang)
        t[:, K_COS + tok * A_ROPE:K_COS + (tok + 1) * A_ROPE] = np.concatenate([cos, cos], 1)
        t[:, K_SIN + tok * A_ROPE:K_SIN + (tok + 1) * A_ROPE] = np.concatenate([-sin, sin], 1)
        for kind in range(2):
            for h in range(B_HEADS):
                t[:, K_FAC + kind * 16 + tok * 8 + h] = HD ** -0.5 / SLOPES[2 * h + kind]
                t[:, K_FAC + kind * 16 + tok * 8 + 4 + h] = 1.0
    return t


class Event:

    def __init__(self, sem, per_layer, start=0):
        self.sem, self.per_layer, self.start = sem, per_layer, start

    def at(self, l, n):
        return l * self.per_layer + (n + self.start)


class Chain:

    def __init__(self, eng, event, l):
        self.eng, self.event, self.l, self.n = eng, event, l, 0

    def __call__(self, ins):
        ins.then_inc(self.event.sem, 1)
        self.n += 1
        self.eng.wait_ge(self.event.sem, self.event.at(self.l, self.n))


def slab_words(s):
    if s < S_GATE0:
        return KGRP[s % 3][1] * CW
    return 2 * Q_RANK if S_UQ <= s < S_UKV else SLAB


def gate_slab_no(g):
    return S_GATE0 + g if g < 2 else S_GATE1 + g - 2


def gate_bank(g):
    return 4 + g if g < 2 else g % 3 if g < 6 else g % 2


def raw_level(s):
    two = [S_BR + 1, S_BR + 3] + [S_FF + k for k in range(NS - S_FF) if k < 4 or (k < 31 and k % 3 != 1)]
    return 16 * sum(2 if n in two else 1 for n in range(s % RING, s + 1, RING))


HEADS = [("b", h) for h in range(B_HEADS)] + [("a", h) for h in range(A_HEADS)] + [("c", h) for h in range(C_HEADS)]
NH = len(HEADS)


def head_slope(kind, h):
    return 1.0 if kind == "a" else SLOPES[2 * h + (kind == "c")]


BR_BANKS = ((4, 6, 2), (0, 2, 4))
PAIR_Y = [4, 5, 0, 1, 2, 3, 6, 7]
GATE_STEPS = [1, 3, 5, 8, 10, 12, 15, 18]
GATE_AT = {GATE_STEPS[2 * i + 1]: 8 + i for i in range(4)}
DVE_LINKS = 88
ACT_LINKS = 6


def build(nc, x, c, w_ada, b_ada, norm1, w_in, g_cq, w_uq, g_ckv, w_ukv, qn_mla, kn_mla, qn_moba, kn_moba,
          qn_dsa, kn_dsa, w_br_a, w_br_b, w_br_c, w_out, norm2, w_gu, w_down, const, out):
    with ExitStack() as ctx:
        def sb(name, shape, dt=F32):
            return ctx.enter_context(nc.sbuf_tensor(name, shape, dt))

        def event(name, per_layer, start=0):
            return Event(ctx.enter_context(nc.semaphore(name)), per_layer, start)

        raw = sb("raw", [P, RING, SLAB])
        w_hi = sb("w_hi", [P, RING, SLAB], F32R)
        w_lo = sb("w_lo", [P, RING, SLAB], F32R)
        x_t = sb("x_t", [P, KT, T])
        h_hi = sb("h_hi", [P, KT, T], F32R)
        h_lo = sb("h_lo", [P, KT, T], F32R)
        proj = sb("proj", [P, TT, C_G])
        y_hi = sb("y_hi", [P, KT, T], F32R)
        y_lo = sb("y_lo", [P, KT, T], F32R)
        front = sb("front", [P, 2 * A_HEADS + 4 + 12, T])
        kz_t = sb("kz_t", [P, 8, T])
        acc = sb("acc", [P, 3072])
        ikz = sb("ikz", [P, 4, T])
        score = sb("score", [P, P + T])
        sel_nd = sb("sel_nd", [P, P + T])
        konst = sb("konst", [P, K_ALL])
        gains = sb("gains", [P, 2 * A_QK + 4 * HD])
        cols = sb("cols", [P, DEPTH, ROWS])
        ones = sb("ones", [P, P])
        rstd = sb("rstd", [P, T])
        cond = sb("cond", [P, KT])
        cond_now = sb("cond_now", [P, 2])
        mod_b = sb("mod_b", [P, 24])
        mod_a = sb("mod_a", [P, 24])
        pcol = sb("pcol", [P, ROWS])
        small = sb("small", [P, 96])
        krr = sb("krr", [P, TT, A_ROPE])
        krw = sb("krw", [P, TT, A_ROPE])

        eps = small[:, 0:1]
        ssc = small[:, 1:5]
        krss = small[:, 5:7]
        rowmax = [small[:, 8 + 8 * i:10 + 8 * i] for i in range(2)]
        negmax = [small[:, 10 + 8 * i:12 + 8 * i] for i in range(2)]
        rowsum = [small[:, 12 + 8 * i:14 + 8 * i] for i in range(2)]
        rinv = [small[:, 14 + 8 * i:16 + 8 * i] for i in range(2)]
        top8 = small[:, 24:32]
        ss16 = small[:, 32:48]
        ss16b = small[:, 64:80]

        qk_t = front[:, 0:16, :]
        pq_t = front[:, 16:20, :]
        own = front[:, 20:32, :].rearrange("p a b -> p (a b)")
        sq = acc[:, 0:1536]
        mod_rows_sb = acc[:, 0:1024]
        relu_b = [acc[:, 1536 + 384 * i:1536 + 384 * (i + 1)] for i in range(4)]
        p_sb = [acc[:, 384 * i:384 * (i + 1)] for i in range(4)]
        pt_sb = [acc[:, 2304 + 384 * i:2304 + 384 * (i + 1)] for i in range(2)]
        q_a = own[:, 0:1536]
        k_a = own[:, 1536:3072]
        iq_t = own[:, 2048:3072].rearrange("p (j t) -> p j t", j=4)
        ik_rep = rstd[:, :].rearrange("p (t m) -> p t m", t=TT)
        ada_raw = [front[:, 12 * i:12 * (i + 1), :].rearrange("p a b -> p (a b)") for i in range(2)]
        ada_pro = [qk_t[:, 0:8, :].rearrange("p a b -> p (a b)"), qk_t[:, 8:16, :].rearrange("p a b -> p (a b)"),
                   own[:, 0:2048]]
        vrows = proj[0:ROWS, 0, 2048:2048 + DEPTH * P].rearrange("r (l m) -> r l m", l=DEPTH)
        ident = konst[:, K_ID:K_ID + P]
        causal = konst[:, K_CM:K_CM + P + T]
        neg_dist = konst[:, K_ND:K_ND + P + T]
        k_nope = proj[:, :, 0:1024].rearrange("p t (h e) -> p t h e", h=A_HEADS)[:, :, :, 0:A_NOPE]
        silu_g = [proj[:, 0, 512 * i:512 * (i + 1)] for i in range(2)]
        glu = [proj[:, 1, 512 * i:512 * (i + 1)] for i in range(2)]
        yh, yl = y_hi[:, :, :].rearrange("p a b -> p (a b)"), y_lo[:, :, :].rearrange("p a b -> p (a b)")
        glu_hi = [yh[:, 512 * i:512 * (i + 1)] for i in range(2)]
        glu_lo = [yl[:, 512 * i:512 * (i + 1)] for i in range(2)]

        def norm_pair(p):
            at = 1024 + (p % 2) * 512
            return proj[:, p // 2, at:at + 512]

        def norm_tile(k):
            return norm_pair(k // 2)[:, (k % 2) * T:(k % 2 + 1) * T]

        def merged(hf):
            return proj[:, hf, 0:1024]

        def gate(g):
            if g < 6:
                at = [C_IQ, 1024, C_C][g // 2]
                return proj[:, g % 2, at:at + 512]
            return own[:, (g - 6) * 512:(g - 5) * 512]

        bank = [ctx.enter_context(nc.psum_tensor(f"bank{i}", [P, 512], F32)) for i in range(8)]

        x_in = event("x_in", 0)
        konst_in = event("konst_in", 0)
        vrows_in = event("vrows_in", 0)
        ones_ok = event("ones_ok", 0)
        zeros_ok = event("zeros_ok", 0)
        x_tp = event("x_tp", 0)
        cols_tp = event("cols_tp", 0)
        cols_ok = event("cols_ok", 0)
        cond_done = event("cond_done", 0)
        apro_in = [event(f"apro_in{i}", 0) for i in range(3)]
        raw_in = [event(f"raw_in{i}", raw_level(NS - RING + i)) for i in range(RING)]
        gains_in = event("gains_in", 16 * 6)
        hi_ready = event("hi_ready", NS)
        lo_ready = event("lo_ready", NS, RING)
        slab_used = event("slab_used", NS, RING)
        ada_in = [event(f"ada_in{i}", 16 * 4 + 32 * 4) for i in range(2)]
        ada_used = event("ada_used", 16, KT)
        acc_zero = event("acc_zero", 2, 1)
        cond_ok = event("cond_ok", 8)
        x_done = event("x_done", 16, 8)
        sq_done = event("sq_done", 8)
        ss_done = event("ss_done", 2)
        std_done = event("std_done", 2)
        hn_done = event("hn_done", 16)
        hhi_done = event("hhi_done", 16)
        hlo_done = event("hlo_done", 16)
        coef_done = event("coef_done", 2)
        chunk_out = event("chunk_out", 2 * CHUNKS, 4)
        ikrep_done = event("ikrep_done", 2)
        idx_tp = event("idx_tp", 1)
        iqt_done = event("iqt_done", 2)
        ikz_done = event("ikz_done", 4)
        mod_rows = event("mod_rows", 2, 1)
        mod_rows_out = event("mod_rows_out", 4, 2)
        mod_tp = event("mod_tp", 2, 1)
        mod_got = event("mod_got", 2, 1)
        cq_tp = event("cq_tp", 1)
        cq_hi = event("cq_hi", 8)
        cq_lo = event("cq_lo", 8)
        cq_ss = event("cq_ss", 4)
        cq_std = event("cq_std", 2)
        cq_rstd = event("cq_rstd", 1)
        idx_sc = event("idx_sc", IDX_HEADS)
        relu_done = event("relu_done", IDX_HEADS)
        idx_acc = event("idx_acc", 2 * IDX_HEADS)
        kr_done = event("kr_done", 1)
        psq_done = event("psq_done", 2)
        pss_done = event("pss_done", 2)
        pstd_done = event("pstd_done", 2)
        pn_done = event("pn_done", 2)
        pair_tp = event("pair_tp", 2)
        pq_out = event("pq_out", 2)
        kz_out = event("kz_out", 4)
        gate_out = event("gate_out", 12)
        uq_out = event("uq_out", 4)
        ukv_out = event("ukv_out", 4)
        msq_done = event("msq_done", 2)
        mss_done = event("mss_done", 2)
        mstd_done = event("mstd_done", 2)
        mqk_done = event("mqk_done", 2)
        mla_tp = event("mla_tp", 2)
        mla_out_a = event("mla_out_a", 4)
        mla_out_d = event("mla_out_d", 4)
        scored = event("scored", NH)
        maxed = event("maxed", NH)
        ttr_done = event("ttr_done", 2 * NH)
        exped = event("exped", 2 * NH)
        p_ready = event("p_ready", NH)
        p_tp = event("p_tp", NH)
        pt_out = event("pt_out", NH)
        pv_done = event("pv_done", NH)
        y_hi_done = event("y_hi_done", NH // 2)
        y_lo_done = event("y_lo_done", NH // 2)
        m_first = event("m_first", 4)
        m_done = event("m_done", 4)
        m_hi = event("m_hi", 4)
        m_lo = event("m_lo", 4)
        silu_done = event("silu_done", FG)
        glu_done = event("glu_done", FG, 1)
        glu_hi_done = event("glu_hi_done", FG)
        glu_lo_done = event("glu_lo_done", FG)
        dve_pro = event("dve_pro", 0)
        dve_chain = event("dve_chain", DVE_LINKS)
        act_chain = event("act_chain", ACT_LINKS)
        out_tp = event("out_tp", 0)
        out_rows = event("out_rows", 0)
        out_stored = event("out_stored", 0)
        waited = event("waited", 0)

        block = ctx.enter_context(nc.Block())

        def apart(eng):
            eng.sem_inc(waited.sem, 1)

        @block.sync
        def _(sp):
            for l in range(DEPTH):
                sp.dma_start(vrows[R_C:R_C + 8, l, :], c[0].rearrange("(r m) -> r m", m=P)).then_inc(vrows_in.sem, 16)
            sp.wait_ge(vrows_in.sem, 16 * (5 + DEPTH))
            for k in range(KT):
                if k == 3:
                    sp.dma_start(proj[:, :, 0:D], x[0].rearrange("(t p) d -> p t d", p=P)).then_inc(x_in.sem, 16)
                if k >= 3:
                    sp.wait_ge(ada_used.sem, k - 2)
                sp.dma_start(ada_pro[k % 3], w_ada[0, k * P:(k + 1) * P, 0:2 * D]).then_inc(apro_in[k % 3].sem, 16)
            with sp.Fori(0, DEPTH) as l:
                def load(s0, step, *parts):
                    sp.wait_ge(lo_ready.sem, lo_ready.at(l, step + (s0 + 1 - RING)))
                    apart(sp)
                    for dst, src in parts:
                        sp.dma_start(dst, src).then_inc(raw_in[s0 % RING].sem, 16)

                def rows(w, k0, k, c0, n):
                    return w.rearrange("l (c p) n -> l p c n", p=P)[l, :, k0:k0 + k, ds(c0, n)]

                def slot_view(s0, k, n, at=0):
                    return raw[:, s0 % RING, at:at + k * n].rearrange("p (c n) -> p c n", c=k)

                def chunk_pair(i):
                    for cc in range(2):
                        for j, (k0, k) in enumerate(KGRP):
                            load(3 * cc + j, 6 * i, (slot_view(j, k, CW), rows(
                                w_in, k0, k, (CHUNKS - 1 - cc) * CW - 2 * CW * i, CW)))

                with sp.Fori(0, CHUNKS // 2 - 1) as i:
                    chunk_pair(i)
                sp.wait_ge(coef_done.sem, coef_done.at(l, 1))
                apart(sp)
                at = 0
                for src, n in ((qn_mla, A_QK), (kn_mla, A_QK), (qn_moba, HD), (kn_moba, HD), (qn_dsa, HD),
                               (kn_dsa, HD)):
                    sp.dma_start(gains[:, at:at + n], src[l].partition_broadcast(P)).then_inc(gains_in.sem, 16)
                    at += n
                chunk_pair(CHUNKS // 2 - 1)

                def load_gates(s, g):
                    load(s, 0, (slot_view(s, KT, 256), rows(w_in, 0, KT, C_G + 256 * g, 256)))

                for g in range(2):
                    load_gates(gate_slab_no(g), g)
                for j in range(3):
                    load(S_UQ + j, 0, (slot_view(S_UQ + j, 2, Q_RANK), rows(w_uq, 2 * j, 2, 0, Q_RANK)))
                load(S_UKV, 0, (slot_view(S_UKV, 2, D), rows(w_ukv, 0, 2, 0, D)))
                for g in range(2, 12):
                    load_gates(gate_slab_no(g), g)
                for hf in range(2):
                    s = S_BR + 2 * hf
                    load(s, 0, (slot_view(s, 4, 512), rows(w_br_a, 0, 4, 512 * hf, 512)))
                    load(s + 1, 0, (slot_view(s + 1, 2, 512), rows(w_br_b, 0, 2, 512 * hf, 512)),
                         (slot_view(s + 1, 2, 512, 1024), rows(w_br_c, 0, 2, 512 * hf, 512)))
                for o in range(4):
                    load(S_OUT + o, 0, (slot_view(S_OUT + o, 4, 512), rows(w_out, 4 * (o // 2), 4, 512 * (o % 2), 512)))

                def load_gu(s0, step, i):
                    for kg in range(2):
                        v = raw[:, (s0 + kg) % RING, :].rearrange("p (c e n) -> p c e n", c=4, e=2)
                        load(s0 + kg, step, (v[:, :, 0, :], rows(w_gu, 4 * kg, 4, 256 * i, 256)),
                             (v[:, :, 1, :], rows(w_gu, 4 * kg, 4, 256 * i + D_FF, 256)))

                def load_down(s0, step, i):
                    load(s0, step, (slot_view(s0, 2, D), w_down.rearrange("l (c p) n -> l p c n", p=P)[l, :, ds(2 * i, 2), :]))

                load_gu(S_FF, 0, 0)
                load_gu(S_FF + 2, 0, 1)
                load_down(S_FF + 4, 0, 0)
                with sp.Fori(0, FF_PAIRS) as b:
                    for e in range(2):
                        load_gu(S_FFL + 3 * e, 6 * b, 2 * b + (e + 2))
                        load_down(S_FFL + 3 * e + 2, 6 * b, 2 * b + (e + 1))
                load_gu(S_FFE, 0, FG - 1)
                load_down(S_FFE + 2, 0, FG - 2)
                load_down(S_FFE + 3, 0, FG - 1)

            sp.wait_ge(out_rows.sem, 4)
            sp.dma_start(out[0].rearrange("(t p) d -> p t d", p=P), proj[:, :, 0:D]).then_inc(out_stored.sem, 16)
            sp.wait_ge(out_stored.sem, 16)

        @block.gpsimd
        def _(pool):
            nc.gpsimd.memset(ones[:], 1.0).then_inc(ones_ok.sem, 1)
            nc.gpsimd.memset(acc[:], 0.0).then_inc(acc_zero.sem, 1)
            nc.gpsimd.memset(eps, EPS).then_inc(zeros_ok.sem, 1)
            nc.gpsimd.memset(kz_t[:], 0.0).then_inc(zeros_ok.sem, 1)
            nc.gpsimd.memset(ikz[:], 0.0).then_inc(zeros_ok.sem, 1)
            pool.wait_ge(ada_used.sem, KT)
            with pool.Fori(0, DEPTH) as l:
                def load_ada(m, e, *parts):
                    pool.wait_ge(ada_used.sem, ada_used.at(l, m - 1))
                    apart(pool)
                    for dst, src in parts:
                        pool.dma_start(dst, src).then_inc(ada_in[e].sem, 16)

                pool.wait_ge(mod_tp.sem, mod_tp.at(l, 0))
                apart(pool)
                nc.gpsimd.memset(acc[:], 0.0).then_inc(acc_zero.sem, 1)
                with pool.Fori(0, KT // 2) as i:
                    for e in range(2):
                        load_ada(2 * i + e, e, (ada_raw[e], w_ada[l, ds(P * (2 * i + e), P), ADA_T0:ADA_T0 + ADA_TN]))
                pool.wait_ge(pv_done.sem, pv_done.at(l, NH))
                apart(pool)
                nc.gpsimd.memset(acc[:], 0.0).then_inc(acc_zero.sem, 1)
                pool.wait_ge(m_done.sem, m_done.at(l, 4))
                apart(pool)
                nxt = (l + 1) % DEPTH
                with pool.Fori(0, KT // 2) as i:
                    for e in range(2):
                        k = 2 * i + e
                        load_ada(k + KT, e, (ada_raw[e][:, 0:D], w_ada[l, ds(P * k, P), 5 * D:6 * D]),
                                 (ada_raw[e][:, D:3 * D], w_ada[nxt, ds(P * k, P), 0:2 * D]))

        @block.tensor
        def _(pe):
            pe.wait_ge(konst_in.sem, 16)
            pe.wait_ge(vrows_in.sem, 16 * (5 + DEPTH))
            for l in range(DEPTH):
                last = nc.tensor.transpose(bank[4][:, l * ROWS:(l + 1) * ROWS], vrows[:, l, :], ident[0:ROWS, 0:ROWS])
            last.then_inc(cols_tp.sem, 1)
            pe.wait_ge(x_in.sem, 16)
            for k in range(KT):
                for t in range(TT):
                    at = (k % 2) * T + t * P
                    last = nc.tensor.transpose(bank[k // 2][:, at:at + P], proj[:, t, k * P:(k + 1) * P], ident)
                if k % 2:
                    last.then_inc(x_tp.sem, 1)
            pe.wait_ge(ones_ok.sem, 1)
            pe.sem_inc(slab_used.sem, RING)

            def mod_columns(l, n, mods, used, between=None):
                pe.wait_ge(ada_used.sem, used)
                for j in range(6):
                    b, q = 6 + j // 4, 32 * (j % 4)
                    last = nc.tensor.matmul(bank[b][q:q + 32, :], ones[:, 0:32], acc[:, 512 * j:512 * (j + 1)],
                                            start=True, stop=True)
                last.then_inc(mod_rows.sem, 1)
                if between:
                    between()
                pe.wait_ge(mod_rows_out.sem, mods)
                for b in range(4):
                    nc.tensor.transpose(bank[6][:, P * b:P * (b + 1)], mod_rows_sb[:, P * b:P * (b + 1)], ident)
                for b in range(4):
                    last = nc.tensor.transpose(bank[7][:, 64 * b:64 * (b + 1)],
                                               mod_rows_sb[0:64, 512 + P * b:512 + P * (b + 1)], ident[0:64, 0:64])
                last.then_inc(mod_tp.sem, 1)

            mod_columns(0, 0, 2, KT)

            def slab(l, s0, step=0):
                pe.wait_ge(lo_ready.sem, lo_ready.at(l, step + (s0 + 1)))

            def passes(b_out, st_hi, st_lo, mv_hi, mv_lo, start, stop):
                nc.tensor.matmul(b_out, st_hi, mv_hi, start=start, stop=False, skip_group_check=True)
                nc.tensor.matmul(b_out, st_hi, mv_lo, start=False, stop=False, skip_group_check=True)
                return nc.tensor.matmul(b_out, st_lo, mv_hi, start=False, stop=stop, skip_group_check=True)

            def channel_slab(s0, tiles, first, final):
                slot = s0 % RING
                for o, col, offs, act_hi, act_lo, opens in tiles:
                    for n, off in enumerate(offs):
                        last = passes(o, w_hi[:, slot, off + col:off + col + P],
                                      w_lo[:, slot, off + col:off + col + P], act_hi[n], act_lo[n],
                                      first and opens and n == 0, final and n == len(offs) - 1)
                return last

            def norm_sums(l, which, b):
                for p in range(4):
                    pe.wait_ge(sq_done.sem, sq_done.at(l, 4 * which + p + 1))
                    for e in range(2):
                        last = nc.tensor.matmul(bank[b][:, 0:T], ones[:, :], norm_pair(p)[:, e * T:(e + 1) * T],
                                                start=(p == 0 and e == 0), stop=(p == 3 and e == 1))
                last.then_inc(ss_done.sem, 1)

            def chunks(l, i, which):
                for cc in which:
                    pe.wait_ge(chunk_out.sem, chunk_out.at(l, 4 * i + (2 * cc + 2 - 4)))
                    for j, (k0, n) in enumerate(KGRP):
                        slab(l, 3 * cc + j, 6 * i)
                        for t in range(TT):
                            for kk in range(n):
                                k = k0 + kk
                                if t == 0 and cc == 0:
                                    pe.wait_ge(hlo_done.sem, hlo_done.at(l, k + 1))
                                hh, hl = h_hi[:, k, t * P:(t + 1) * P], h_lo[:, k, t * P:(t + 1) * P]
                                wh = w_hi[:, j, kk * CW:(kk + 1) * CW]
                                wl = w_lo[:, j, kk * CW:(kk + 1) * CW]
                                o = bank[2 * cc + t][:, 0:CW]
                                nc.tensor.matmul(o, hh, wh, start=(k == 0), stop=False)
                                nc.tensor.matmul(o, hl, wh, start=False, stop=False)
                                last = nc.tensor.matmul(o, hh, wl, start=False, stop=(k == KT - 1))
                        last.then_inc(slab_used.sem, 1)

            def gate_slab(l, g, tiles=(0, 1)):
                s = gate_slab_no(g)
                slab(l, s)
                if g >= 5:
                    pe.wait_ge(gate_out.sem, gate_out.at(l, g - 2 if g < 8 else g - 1))
                hi, lo = [h_hi[:, k, :] for k in range(KT)], [h_lo[:, k, :] for k in range(KT)]
                last = channel_slab(s, [(bank[gate_bank(g)][:, m * T:(m + 1) * T], m * P, [256 * k for k in range(KT)],
                                         hi, lo, m == 0) for m in tiles], True, True)
                if 1 in tiles:
                    last.then_inc(slab_used.sem, 1)

            def token_slab(l, s, n_k, k0, width, n_chunk, cw, b0, first, final):
                slot = s % RING
                for t in range(TT):
                    for ch in range(n_chunk):
                        for kk in range(n_k):
                            a_hi = y_hi[:, k0 + kk, t * P:(t + 1) * P]
                            a_lo = y_lo[:, k0 + kk, t * P:(t + 1) * P]
                            at = kk * width + ch * cw
                            o = bank[b0 + n_chunk * t + ch][:, 0:cw]
                            nc.tensor.matmul(o, a_hi, w_hi[:, slot, at:at + cw], start=(first and kk == 0), stop=False)
                            nc.tensor.matmul(o, a_lo, w_hi[:, slot, at:at + cw], start=False, stop=False)
                            last = nc.tensor.matmul(o, a_hi, w_lo[:, slot, at:at + cw], start=False,
                                                    stop=(final and kk == n_k - 1))
                last.then_inc(slab_used.sem, 1)

            with pe.Fori(0, DEPTH) as l:
                norm_sums(l, 0, 4)
                with pe.Fori(0, CHUNKS // 2 - 1) as i:
                    chunks(l, i, (0, 1))
                chunks(l, CHUNKS // 2 - 1, (0,))

                pe.wait_ge(ikrep_done.sem, ikrep_done.at(l, 2))
                pe.wait_ge(chunk_out.sem, chunk_out.at(l, 12))
                for j in range(4):
                    for t in range(TT):
                        at = (j % 2) * T + t * P
                        nc.tensor.transpose(bank[4 + j // 2][:, at:at + P],
                                            proj[:, t, C_IQ + j * P:C_IQ + (j + 1) * P], ident)
                for t in range(TT):
                    last = nc.tensor.transpose(bank[6][:, t * P:(t + 1) * P], ik_rep[:, t, :], ident)
                last.then_inc(idx_tp.sem, 1)

                chunks(l, CHUNKS // 2 - 1, (1,))

                pe.wait_ge(chunk_out.sem, chunk_out.at(l, 2 * CHUNKS))
                for k in range(KT):
                    for t in range(TT):
                        at = (k % 2) * T + t * P
                        last = nc.tensor.transpose(bank[k // 2][:, at:at + P], proj[:, t, k * P:(k + 1) * P], ident)
                last.then_inc(cq_tp.sem, 1)
                pe.wait_ge(iqt_done.sem, iqt_done.at(l, 2))
                gate_slab(l, 0)
                pe.wait_ge(ikz_done.sem, ikz_done.at(l, 4))
                mod_columns(l, 1, mod_rows_out.at(l, 2), ada_used.at(l, KT), lambda: gate_slab(l, 1))
                pe.wait_ge(cq_lo.sem, cq_lo.at(l, KT))
                for j in range(3):
                    slab(l, S_UQ + j)
                    token_slab(l, S_UQ + j, 2, 2 * j, Q_RANK, 2, 384, 0, j == 0, j == 2)

                pe.wait_ge(gate_out.sem, gate_out.at(l, 2))
                pe.wait_ge(mod_got.sem, mod_got.at(l, 1))
                for h in range(IDX_HEADS):
                    if h == IDX_HEADS // 2:
                        slab(l, S_UKV)
                        pe.wait_ge(uq_out.sem, uq_out.at(l, 4))
                        token_slab(l, S_UKV, 2, 6, D, 2, 512, 0, True, True)
                    if h >= 4:
                        pe.wait_ge(relu_done.sem, relu_done.at(l, h - 3))
                    b = 4 + h % 4
                    nc.tensor.matmul(bank[b][:, 0:P], iq_t[:, h // 4, 0:P], ikz[:, h % 4, 0:P], start=True, stop=True)
                    nc.tensor.matmul(bank[b][:, P:P + T], iq_t[:, h // 4, P:T], ikz[:, h % 4, :], start=True,
                                     stop=True).then_inc(idx_sc.sem, 1)
                pe.wait_ge(relu_done.sem, relu_done.at(l, IDX_HEADS))

                for kind, base in ((0, C_C), (1, C_B)):
                    pe.wait_ge(pn_done.sem, pn_done.at(l, kind + 1))
                    for j in range(4):
                        for t in range(TT):
                            at = (j % 2) * T + t * P
                            last = nc.tensor.transpose(bank[4 + 2 * kind + j // 2][:, at:at + P],
                                                       proj[:, t, base + j * P:base + (j + 1) * P], ident)
                    last.then_inc(pair_tp.sem, 1)

                pe.wait_ge(ukv_out.sem, ukv_out.at(l, 4))
                for g in range(2, 6):
                    gate_slab(l, g)

                pe.wait_ge(pq_out.sem, pq_out.at(l, 2))
                pe.wait_ge(kz_out.sem, kz_out.at(l, 4))
                for kind, src in ((0, q_a), (1, k_a)):
                    pe.wait_ge(mqk_done.sem, mqk_done.at(l, kind + 1))
                    if kind:
                        pe.wait_ge(mla_out_a.sem, mla_out_a.at(l, 2))
                        pe.wait_ge(mla_out_d.sem, mla_out_d.at(l, 2))
                    for h in range(A_HEADS):
                        for t in range(TT):
                            at = (h % 2) * T + t * P
                            m = (t * A_HEADS + h) * A_QK
                            last = nc.tensor.transpose(bank[4 + h // 2][0:A_QK, at:at + P], src[:, m:m + A_QK], ident)
                    last.then_inc(mla_tp.sem, 1)
                    gate_slab(l, 6 + kind)
                pe.wait_ge(mla_out_a.sem, mla_out_a.at(l, 4))
                pe.wait_ge(mla_out_d.sem, mla_out_d.at(l, 4))

                def scores(n):
                    kind, h = HEADS[n]
                    if kind == "a":
                        q, k = qk_t[0:A_QK, h, :], qk_t[0:A_QK, A_HEADS + h, :]
                    else:
                        j = (0 if kind == "c" else 1)
                        q, k = pq_t[:, 2 * j + h // 2, :], kz_t[:, 4 * j + h, :]
                    if n >= 2:
                        pe.wait_ge(ttr_done.sem, ttr_done.at(l, 2 * (n - 1)))
                    b = bank[4 + n % 2]
                    nc.tensor.matmul(b[:, 0:P], q[:, 0:P], k[:, 0:P], start=True, stop=True)
                    nc.tensor.matmul(b[:, P:P + T], q[:, P:T], k[:, :], start=True, stop=True).then_inc(scored.sem, 1)

                def turn_p(n):
                    pe.wait_ge(p_ready.sem, p_ready.at(l, n + 1))
                    if n >= 2:
                        pe.wait_ge(pt_out.sem, pt_out.at(l, n - 1))
                    for j in range(3):
                        last = nc.tensor.transpose(bank[6 + n % 2][:, j * P:(j + 1) * P],
                                                   p_sb[n % 4][:, j * P:(j + 1) * P], ident)
                    last.then_inc(p_tp.sem, 1)

                def weigh_v(n):
                    kind, h = HEADS[n]
                    at = {"a": P * h + A_NOPE, "b": C_BV + HD * h, "c": C_CV + HD * h}[kind]
                    pair = n // 2
                    if n % 2 == 0 and pair >= 2:
                        pe.wait_ge(y_lo_done.sem, y_lo_done.at(l, pair - 1))
                    pe.wait_ge(pt_out.sem, pt_out.at(l, n + 1))
                    r, y = HD * (n % 2), bank[2 + pair % 2]
                    nc.tensor.matmul(y[r:r + HD, 0:T], proj[:, 0, at:at + HD], pt_sb[n % 2][:, 0:T],
                                     start=True, stop=False, skip_group_check=True)
                    nc.tensor.matmul(y[r:r + HD, P:T], proj[:, 1, at:at + HD],
                                     pt_sb[n % 2][:, T:T + P], start=False, stop=True,
                                     skip_group_check=True).then_inc(pv_done.sem, 1)

                scores(0)
                for n in range(NH + 3):
                    if n + 1 < NH:
                        scores(n + 1)
                    if 2 <= n <= NH + 1:
                        turn_p(n - 2)
                    if n >= 3:
                        weigh_v(n - 3)
                    if n in GATE_STEPS:
                        half = GATE_STEPS.index(n)
                        gate_slab(l, 8 + half // 2, (half % 2,))

                for hf in range(2):
                    banks = BR_BANKS[hf]

                    def branch(b0, s, base, k0, n_k):
                        hi, lo = [y_hi[:, k0 + k, :] for k in range(n_k)], [y_lo[:, k0 + k, :] for k in range(n_k)]
                        return channel_slab(s, [(bank[b0 + m // 2][:, (m % 2) * T:(m % 2 + 1) * T], m * P,
                                                 [base + 512 * k for k in range(n_k)], hi, lo, m % 2 == 0)
                                                for m in range(4)], True, True)

                    s = S_BR + 2 * hf
                    pe.wait_ge(y_lo_done.sem, y_lo_done.at(l, (B_HEADS + A_HEADS) // 2))
                    if hf:
                        pe.wait_ge(gate_out.sem, gate_out.at(l, 12))
                    slab(l, s)
                    branch(banks[0], s, 0, 0, 4).then_inc(slab_used.sem, 1)
                    slab(l, s + 1)
                    if hf:
                        pe.wait_ge(m_done.sem, m_done.at(l, 2))
                    branch(banks[1], s + 1, 0, 4, 2)
                    pe.wait_ge(y_lo_done.sem, y_lo_done.at(l, NH // 2))
                    branch(banks[2], s + 1, 1024, 6, 2).then_inc(slab_used.sem, 1)

                for o in range(4):
                    kh, ch = o // 2, o % 2
                    pe.wait_ge(m_lo.sem, m_lo.at(l, 2 * kh + 2))
                    if o == 1:
                        pe.wait_ge(m_first.sem, m_first.at(l, 4))
                    slab(l, S_OUT + o)
                    hi, lo = [h_hi[:, 4 * kh + k, :] for k in range(4)], [h_lo[:, 4 * kh + k, :] for k in range(4)]
                    channel_slab(S_OUT + o, [(bank[(6, 0)[ch] + m // 2][:, (m % 2) * T:(m % 2 + 1) * T], m * P,
                                              [512 * k for k in range(4)], hi, lo, m % 2 == 0) for m in range(4)],
                                 kh == 0, kh == 1).then_inc(slab_used.sem, 1)

                norm_sums(l, 1, 2)

                def gate_up(s0, step, par, i, fresh=False):
                    pe.wait_ge(glu_done.sem, glu_done.at(l, i - 1))
                    for kg in range(2):
                        slab(l, s0 + kg, step)
                        for pairs in ((0,), (1,)) if fresh else ((0, 1),):
                            if fresh:
                                pe.wait_ge(hlo_done.sem, hlo_done.at(l, KT + 4 * kg + 2 * pairs[0] + 2))
                            ks = [2 * q + e for q in pairs for e in range(2)]
                            hi, lo = [h_hi[:, 4 * kg + k, :] for k in ks], [h_lo[:, 4 * kg + k, :] for k in ks]
                            last = channel_slab(s0 + kg, [(bank[4 + 2 * par + e][:, m * T:(m + 1) * T], 256 * e + m * P,
                                                           [512 * k for k in ks], hi, lo, m == 0)
                                                          for e in range(2) for m in range(2)],
                                                kg == 0 and 0 in pairs, kg == 1 and 1 in pairs)
                        last.then_inc(slab_used.sem, 1)

                def down(s0, step, par, i, first=False, final=False):
                    pe.wait_ge(glu_lo_done.sem, glu_lo_done.at(l, i + 1))
                    slab(l, s0, step)
                    hi = [glu_hi[par][:, k * T:(k + 1) * T] for k in range(2)]
                    lo = [glu_lo[par][:, k * T:(k + 1) * T] for k in range(2)]
                    channel_slab(s0, [(bank[m // 2][:, (m % 2) * T:(m % 2 + 1) * T], m * P, [0, D], hi, lo, m % 2 == 0)
                                      for m in range(KT)], first, final).then_inc(slab_used.sem, 1)

                gate_up(S_FF, 0, 0, 1, fresh=True)
                gate_up(S_FF + 2, 0, 1, 1)
                down(S_FF + 4, 0, 0, 0, first=True)
                with pe.Fori(0, FF_PAIRS) as b:
                    for e in range(2):
                        gate_up(S_FFL + 3 * e, 6 * b, e, 2 * b + (e + 2))
                        down(S_FFL + 3 * e + 2, 6 * b, (e + 1) % 2, 2 * b + (e + 1))
                gate_up(S_FFE, 0, 0, FG - 1)
                pe.wait_ge(glu_done.sem, glu_done.at(l, FG - 1))
                mod_columns(l, 2, mod_rows_out.at(l, 4), ada_used.at(l, 2 * KT))
                down(S_FFE + 2, 0, 1, FG - 2)
                down(S_FFE + 3, 0, 0, FG - 1, final=True)

            pe.wait_ge(x_done.sem, x_done.at(DEPTH, 0))
            for t in range(TT):
                for k in range(KT):
                    last = nc.tensor.transpose(bank[2 * t + k // 4][:, (k % 4) * P:(k % 4 + 1) * P],
                                               x_t[:, k, t * P:(t + 1) * P], ident)
                    if k % 4 == 3:
                        last.then_inc(out_tp.sem, 1)

        @block.scalar
        def _(act):
            act.sem_inc(chunk_out.sem, 4)
            nc.scalar.dma_start(konst[:], const).then_inc(konst_in.sem, 16)
            for src, at, n in ((b_ada, 0, 48), (norm1, R_N1, 8), (norm2, R_N2, 8), (g_cq, R_GQ, 6), (g_ckv, R_GKV, 2)):
                nc.scalar.dma_start(vrows[at:at + n, :, :], src.rearrange("l (r m) -> r l m", m=P))\
                    .then_inc(vrows_in.sem, 16)
            act.wait_ge(cols_tp.sem, 1)
            nc.scalar.activation(cols[:, :, :].rearrange("p l r -> p (l r)"), bank[4][:, 0:DEPTH * ROWS],
                                 ACT.Copy).then_inc(cols_ok.sem, 1)
            act.wait_ge(cols_ok.sem, 1)
            nc.scalar.activation(cond[:], cols[:, 0, R_C:R_C + KT], ACT.Silu).then_inc(cond_done.sem, 1)
            for b in range(4):
                act.wait_ge(x_tp.sem, b + 1)
                nc.scalar.activation(x_t[:, 2 * b:2 * b + 2, :].rearrange("p a t -> p (a t)"), bank[b][:, :],
                                     ACT.Copy).then_inc(x_done.sem, 2)

            def mod_rows_copy(l, n):
                act.wait_ge(mod_rows.sem, mod_rows.at(l, n))
                nc.scalar.activation(mod_rows_sb[:, 0:512], bank[6][:, :], ACT.Copy).then_inc(mod_rows_out.sem, 1)
                nc.scalar.activation(mod_rows_sb[0:64, 512:1024], bank[7][0:64, :], ACT.Copy)\
                    .then_inc(mod_rows_out.sem, 1)

            mod_rows_copy(0, 0)

            def hi(l, s0):
                hi_loop(l, s0, 0)

            def hi_loop(l, s0, i):
                slot, n = s0 % RING, slab_words(s0)
                act.wait_ge(raw_in[slot].sem, raw_in[slot].at(l, i * (raw_level(s0 + 6) - raw_level(s0)) + raw_level(s0)))
                act.wait_ge(slab_used.sem, slab_used.at(l, 6 * i + (s0 + 1 - RING)))
                nc.scalar.activation(w_hi[:, slot, 0:n], raw[:, slot, 0:n], ACT.Copy).then_inc(hi_ready.sem, 1)

            def norm(l, which):
                for p in range(4):
                    act.wait_ge(x_done.sem, x_done.at(l, 2 * p + 2 + (8 if which else 0) - 8))
                    nc.scalar.activation(norm_pair(p), x_t[:, 2 * p:2 * p + 2, :].rearrange("p a t -> p (a t)"),
                                         ACT.Square).then_inc(sq_done.sem, 1)
                act.wait_ge(ss_done.sem, ss_done.at(l, which + 1))
                nc.scalar.activation(rstd[:], bank[2 if which else 4][:, 0:T], ACT.Sqrt, bias=eps, scale=1.0 / D)\
                    .then_inc(std_done.sem, 1)
                shift = mod_b[:, 8:16] if which else mod_a[:, 8:16]
                act.wait_ge(coef_done.sem, coef_done.at(l, which + 1))
                for k in range(KT):
                    act.wait_ge(hn_done.sem, hn_done.at(l, KT * which + k + 1))
                    nc.scalar.activation(h_hi[:, k, :], norm_tile(k), ACT.Identity, bias=shift[:, k:k + 1])\
                        .then_inc(hhi_done.sem, 1)

            def chunks(l, i, which, loop):
                for cc in which:
                    last_of_all = not loop and cc == 1
                    for j in range(2 if last_of_all else 3):
                        s = 3 * cc + j + 2
                        hi_loop(l, s, i) if loop else hi(l, 6 * i + s)
                    act.wait_ge(slab_used.sem, slab_used.at(l, 6 * i + 3 * (cc + 1)))
                    for t in range(TT):
                        nc.scalar.activation(proj[:, t, ds((CHUNKS - 1 - cc) * CW - 2 * CW * i, CW)],
                                             bank[2 * cc + t][:, 0:CW], ACT.Copy).then_inc(chunk_out.sem, 1)
                    if last_of_all:
                        hi(l, 6 * i + 3 * cc + 4)

            def gate_act(l, g):
                s = gate_slab_no(g)
                act.wait_ge(slab_used.sem, slab_used.at(l, s + 1))
                nc.scalar.activation(gate(g), bank[gate_bank(g)][:, :], ACT.Tanh, scale=0.5).then_inc(gate_out.sem, 1)

            act.wait_ge(zeros_ok.sem, 3)
            with act.Fori(0, DEPTH) as l:
                link = Chain(act, act_chain, l)
                hi(l, 0)
                hi(l, 1)
                norm(l, 0)
                with act.Fori(0, CHUNKS // 2 - 1) as i:
                    chunks(l, i, (0, 1), True)
                chunks(l, CHUNKS // 2 - 1, (0,), False)
                act.wait_ge(idx_tp.sem, idx_tp.at(l, 1))
                for j in range(2):
                    nc.scalar.activation(iq_t[:, 2 * j:2 * j + 2, :].rearrange("p a t -> p (a t)"), bank[4 + j][:, :],
                                         ACT.Copy).then_inc(iqt_done.sem, 1)
                chunks(l, CHUNKS // 2 - 1, (1,), False)

                act.wait_ge(cq_tp.sem, cq_tp.at(l, 1))
                for k in range(KT):
                    nc.scalar.activation(y_hi[:, k, :], bank[k // 2][:, (k % 2) * T:(k % 2 + 1) * T], ACT.Copy,
                                         scale=pcol[:, R_GQ + k:R_GQ + k + 1]).then_inc(cq_hi.sem, 1)
                hi(l, S_UQ)
                gate_act(l, 0)
                hi(l, S_UQ + 1)
                mod_rows_copy(l, 1)
                act.wait_ge(chunk_out.sem, chunk_out.at(l, 2 * CHUNKS))
                for m, (c0, n) in enumerate(((0, Q_RANK), (Q_RANK, KV_RANK))):
                    for t in range(TT):
                        if m:
                            act.wait_ge(cq_ss.sem, cq_ss.at(l, t + 1))
                        nc.scalar.activation(acc[:, 1536 + Q_RANK * (t % 2):1536 + Q_RANK * (t % 2) + n],
                                             proj[:, t, c0:c0 + n], ACT.Square,
                                             accum_out=ssc[:, 2 * m + t:2 * m + t + 1]).then_inc(cq_ss.sem, 1)
                act.wait_ge(mod_tp.sem, mod_tp.at(l, 1))

                def pair_squares(kind, base):
                    nc.scalar.activation(acc[:, 0:1024].rearrange("p (t n) -> p t n", t=TT),
                                         proj[:, :, base:base + 512], ACT.Square).then_inc(psq_done.sem, 1)

                pair_squares(0, C_C)
                act.wait_ge(cq_ss.sem, cq_ss.at(l, 4))
                for m, n in ((0, Q_RANK), (1, KV_RANK)):
                    nc.scalar.activation(ssc[:, 2 * m:2 * m + 2], ssc[:, 2 * m:2 * m + 2], ACT.Sqrt, bias=eps,
                                         scale=1.0 / n).then_inc(cq_std.sem, 1)
                gate_act(l, 1)
                hi(l, S_UQ + 2)
                act.wait_ge(pss_done.sem, pss_done.at(l, 1))
                pair_squares(1, C_B)
                for kind, ss in ((0, ss16), (1, ss16b)):
                    act.wait_ge(pss_done.sem, pss_done.at(l, kind + 1))
                    nc.scalar.activation(ss, ss, ACT.Sqrt, bias=eps, scale=1.0 / HD).then_inc(pstd_done.sem, 1)
                hi(l, S_UKV)
                hi(l, S_GATE1)

                act.wait_ge(cq_rstd.sem, cq_rstd.at(l, 1))
                act.wait_ge(slab_used.sem, slab_used.at(l, S_UQ + 3))
                for t in range(TT):
                    for ch in range(2):
                        at = t * Q_RANK + 384 * ch
                        nc.scalar.activation(q_a[:, at:at + 384], bank[2 * t + ch][:, 0:384], ACT.Copy,
                                             scale=ssc[:, t:t + 1]).then_inc(uq_out.sem, 1)
                act.wait_ge(uq_out.sem, uq_out.at(l, 4))
                for h in range(IDX_HEADS):
                    if h == 4:
                        nc.scalar.activation(sq, q_a, ACT.Square).then_inc(msq_done.sem, 1)
                        hi(l, S_GATE1 + 1)
                    if h == IDX_HEADS // 2:
                        act.wait_ge(slab_used.sem, slab_used.at(l, S_UKV + 1))
                        for t in range(TT):
                            for ch in range(2):
                                nc.scalar.activation(proj[:, t, 512 * ch:512 * (ch + 1)], bank[2 * t + ch][:, :],
                                                     ACT.Copy, scale=ssc[:, 2 + t:3 + t]).then_inc(ukv_out.sem, 1)
                    act.wait_ge(idx_sc.sem, idx_sc.at(l, h + 1))
                    if h >= 4:
                        act.wait_ge(idx_acc.sem, idx_acc.at(l, 2 * (h - 3)))
                    nc.scalar.activation(relu_b[h % 4], bank[4 + h % 4][:, 0:P + T], ACT.Relu).then_inc(relu_done.sem, 1)
                hi(l, S_GATE1 + 2)
                for kind in range(2):
                    act.wait_ge(pair_tp.sem, pair_tp.at(l, kind + 1))
                    nc.scalar.activation(pq_t[:, 2 * kind:2 * kind + 2, :].rearrange("p a t -> p (a t)"),
                                         bank[4 + 2 * kind][:, :], ACT.Copy).then_inc(pq_out.sem, 1)
                act.wait_ge(ukv_out.sem, ukv_out.at(l, 4))
                act.wait_ge(mss_done.sem, mss_done.at(l, 1))
                nc.scalar.activation(acc[:, 0:1024].rearrange("p (t h d) -> p t h d", t=TT, h=A_HEADS), k_nope,
                                     ACT.Square).then_inc(msq_done.sem, 1)
                nc.scalar.activation(ss16, ss16, ACT.Sqrt, bias=eps, scale=1.0 / A_QK).then_inc(mstd_done.sem, 1)
                act.wait_ge(kr_done.sem, kr_done.at(l, 1))
                gate_act(l, 2)
                hi(l, S_GATE1 + 3)
                act.wait_ge(mss_done.sem, mss_done.at(l, 2))
                nc.scalar.activation(ss16b, ss16b, ACT.Sqrt, bias=eps, scale=1.0 / A_QK).then_inc(mstd_done.sem, 1)
                for g in range(3, 6):
                    gate_act(l, g)
                    hi(l, S_GATE1 + g + 1)
                for kind in range(2):
                    act.wait_ge(mla_tp.sem, mla_tp.at(l, kind + 1))
                    for b in range(2):
                        m = A_HEADS * kind + 2 * b
                        nc.scalar.activation(qk_t[0:A_QK, m:m + 2, :].rearrange("p a t -> p (a t)"),
                                             bank[4 + b][0:A_QK, :], ACT.Copy).then_inc(mla_out_a.sem, 1)
                    if kind == 0:
                        gate_act(l, 6)
                        hi(l, S_GATE1 + 7)
                gate_act(l, 7)

                def expo(n):
                    kind, h = HEADS[n]
                    slope = head_slope(kind, h)
                    act.wait_ge(maxed.sem, maxed.at(l, n + 1))
                    for t, (c0, c1) in enumerate(((0, P), (P, P + T))):
                        nc.scalar.activation(p_sb[n % 4][:, c0:c1], p_sb[n % 4][:, c0:c1], ACT.Exp,
                                             bias=negmax[n % 2][:, t:t + 1], scale=slope,
                                             accum_out=rowsum[n % 2][:, t:t + 1]).then_inc(exped.sem, 1)

                for n in range(NH + 4):
                    if n < NH:
                        expo(n)
                    if 2 <= n <= NH + 1:
                        act.wait_ge(p_tp.sem, p_tp.at(l, n - 1))
                        if n >= 4:
                            act.wait_ge(pv_done.sem, pv_done.at(l, n - 3))
                        nc.scalar.activation(pt_sb[n % 2], bank[6 + n % 2][:, 0:P + T], ACT.Copy)\
                            .then_inc(pt_out.sem, 1)
                    if n >= 5 and n % 2:
                        pair = (n - 5) // 2
                        act.wait_ge(pv_done.sem, pv_done.at(l, 2 * pair + 2))
                        nc.scalar.activation(y_hi[:, PAIR_Y[pair], :], bank[2 + pair % 2][:, 0:T],
                                             ACT.Copy).then_inc(y_hi_done.sem, 1)
                    if n - 1 in GATE_AT:
                        hi(l, gate_slab_no(GATE_AT[n - 1]) + 2)
                        gate_act(l, GATE_AT[n - 1])

                for hf in range(2):
                    for m in range(2):
                        hi(l, S_BR + 2 + 2 * hf + m)
                    for q in range(2):
                        act.wait_ge(m_done.sem, m_done.at(l, 2 * hf + q + 1))
                        k = 4 * hf + 2 * q
                        nc.scalar.activation(h_hi[:, k:k + 2, :].rearrange("p a t -> p (a t)"),
                                             merged(hf)[:, 512 * q:512 * (q + 1)], ACT.Copy, scale=0.5)\
                            .then_inc(m_hi.sem, 1)
                for s in range(S_OUT + 2, S_FF + 2):
                    hi(l, s)
                norm(l, 1)

                def silu_glu(s_last, step, par, i):
                    act.wait_ge(slab_used.sem, slab_used.at(l, step + (s_last + 1)))
                    nc.scalar.activation(silu_g[par], bank[4 + 2 * par][:, :], ACT.Silu).then_inc(silu_done.sem, 1)
                    act.wait_ge(glu_done.sem, glu_done.at(l, i + 1))
                    nc.scalar.activation(glu_hi[par], glu[par], ACT.Copy).then_inc(glu_hi_done.sem, 1)

                hi(l, S_FF + 2)
                silu_glu(S_FF + 1, 0, 0, 0)
                hi(l, S_FF + 3)
                hi(l, S_FF + 4)
                hi(l, S_FF + 5)
                silu_glu(S_FF + 3, 0, 1, 1)
                hi(l, S_FF + 6)
                with act.Fori(0, FF_PAIRS) as b:
                    for e in range(2):
                        hi_loop(l, S_FFL + 3 * e + 2, b)
                        hi_loop(l, S_FFL + 3 * e + 3, b)
                        silu_glu(S_FFL + 3 * e + 1, 6 * b, e, 2 * b + (e + 2))
                        hi_loop(l, S_FFL + 3 * e + 4, b)
                hi(l, S_FFE + 2)
                hi(l, S_FFE + 3)
                silu_glu(S_FFE + 1, 0, 0, FG - 1)
                mod_rows_copy(l, 2)

            for b in range(4):
                act.wait_ge(out_tp.sem, b + 1)
                nc.scalar.activation(proj[:, b // 2, (b % 2) * 512:(b % 2 + 1) * 512], bank[b][:, :], ACT.Copy)\
                    .then_inc(out_rows.sem, 1)

        @block.vector
        def _(dve):
            dve.sem_inc(lo_ready.sem, RING)
            dve.sem_inc(glu_done.sem, 1)
            dve.wait_ge(cond_done.sem, 1)
            dve.wait_ge(acc_zero.sem, 1)
            for k in range(KT):
                dve.wait_ge(apro_in[k % 3].sem, 16 * (k // 3 + 1))
                if k:
                    dve.wait_ge(ada_used.sem, k)
                nc.vector.scalar_tensor_tensor(out=acc[:, D:3 * D], in0=ada_pro[k % 3], scalar=cond[:, k:k + 1],
                                               in1=acc[:, D:3 * D], op0=ALU.mult, op1=ALU.add)\
                    .then_inc(ada_used.sem, 1)

            def mod_get(l, n, mod):
                dve.wait_ge(mod_tp.sem, mod_tp.at(l, n))
                v0 = bank[6][:, :].rearrange("p (b j r) -> p j b r", b=4, j=4, r=32)[:, :, :, 0]
                v1 = bank[7][:, 0:256].rearrange("p (b j r) -> p j b r", b=4, j=2, r=32)[:, :, :, 0]
                link(nc.vector.tensor_copy(mod[:, 0:16].rearrange("p (j b) -> p j b", j=4), v0))
                nc.vector.tensor_copy(mod[:, 16:24].rearrange("p (j b) -> p j b", j=2), v1).then_inc(mod_got.sem, 1)
                dve.wait_ge(mod_got.sem, mod_got.at(l, n))

            link = Chain(dve, dve_pro, 0)
            mod_get(0, 0, mod_a)

            def lo(l, s0, i=0):
                slot, n = s0 % RING, slab_words(s0)
                dve.wait_ge(hi_ready.sem, hi_ready.at(l, 6 * i + (s0 + 1)))
                nc.vector.tensor_tensor(w_lo[:, slot, 0:n], raw[:, slot, 0:n], w_hi[:, slot, 0:n], ALU.subtract)\
                    .then_inc(lo_ready.sem, 1)

            def coefficients(mod, gain_row):
                link(nc.vector.scalar_tensor_tensor(out=mod[:, 16:24], in0=mod[:, 16:24], scalar=1.0,
                                                    in1=pcol[:, gain_row:gain_row + 8], op0=ALU.add, op1=ALU.mult))
                dve.sem_inc(coef_done.sem, 1)

            def norm(l, which):
                dve.wait_ge(std_done.sem, std_done.at(l, which + 1))
                link(nc.vector.reciprocal(rstd[:], rstd[:]))
                scale, shift = (mod_b[:, 16:24], mod_b[:, 8:16]) if which else (mod_a[:, 16:24], mod_a[:, 8:16])


                def scaled(k):
                    nc.vector.scalar_tensor_tensor(out=norm_tile(k), in0=x_t[:, k, :], scalar=scale[:, k:k + 1],
                                                   in1=rstd[:], op0=ALU.mult, op1=ALU.mult).then_inc(hn_done.sem, 1)

                scaled(0)
                for k in range(KT):
                    if k + 1 < KT:
                        scaled(k + 1)
                    dve.wait_ge(hhi_done.sem, hhi_done.at(l, KT * which + k + 1))
                    nc.vector.scalar_tensor_tensor(out=h_lo[:, k, :], in0=norm_tile(k), scalar=shift[:, k:k + 1],
                                                   in1=h_hi[:, k, :], op0=ALU.add, op1=ALU.subtract)\
                        .then_inc(hlo_done.sem, 1)

            def pick_cond(l, i, n, before):
                dve.wait_ge(ada_used.sem, ada_used.at(l, before))
                nc.vector.tensor_copy(cond_now[:], cond[:, ds(2 * i, 2)]).then_inc(cond_ok.sem, 1)
                dve.wait_ge(cond_ok.sem, cond_ok.at(l, n))

            def ada_step(l, m, landed, e):
                dve.wait_ge(ada_in[e].sem, landed)
                dve.wait_ge(ada_used.sem, ada_used.at(l, m))
                nc.vector.scalar_tensor_tensor(out=acc[:], in0=ada_raw[e], scalar=cond_now[:, e:e + 1], in1=acc[:],
                                               op0=ALU.mult, op1=ALU.add).then_inc(ada_used.sem, 1)

            def chunk(l, i, cc):
                for j in range(3):
                    lo(l, 3 * cc + j + 2, i) if not isinstance(i, int) else lo(l, 6 * i + 3 * cc + j + 2)
                ada_step(l, 2 * i + cc, ada_in[cc].at(l, 16 * i + 16), cc)

            with dve.Fori(0, DEPTH) as l:
                link = Chain(dve, dve_chain, l)
                link(nc.vector.tensor_copy(pcol[:].unsqueeze(1), cols[:, ds(l, 1), :]))
                link(nc.vector.tensor_tensor(mod_a[:, 8:24], mod_a[:, 8:24], pcol[:, 0:16], ALU.add))
                coefficients(mod_a, R_N1)
                lo(l, 0)
                lo(l, 1)
                norm(l, 0)
                dve.wait_ge(acc_zero.sem, acc_zero.at(l, 1))
                apart(dve)
                with dve.Fori(0, CHUNKS // 2 - 1) as i:
                    pick_cond(l, i, i + 1, 2 * i)
                    chunk(l, i, 0)
                    chunk(l, i, 1)
                last = CHUNKS // 2 - 1
                pick_cond(l, last, last + 1, 2 * last)
                dve.wait_ge(chunk_out.sem, chunk_out.at(l, 12))
                for t in range(TT):
                    nc.vector.tensor_copy(ik_rep[:, t, :].rearrange("p (r d) -> p r d", r=4),
                                          proj[:, t, C_IK:C_IK + IDX_DIM].unsqueeze(1).to_broadcast([P, 4, IDX_DIM]))\
                        .then_inc(ikrep_done.sem, 1)
                chunk(l, last, 0)
                dve.wait_ge(idx_tp.sem, idx_tp.at(l, 1))
                for r in range(4):
                    q = slice(32 * r, 32 * r + 32)
                    nc.vector.tensor_copy(ikz[q, r, :], bank[6][q, 0:T]).then_inc(ikz_done.sem, 1)
                chunk(l, last, 1)

                for k in range(KT):
                    dve.wait_ge(cq_hi.sem, cq_hi.at(l, 2 * (k // 2) + 2))
                    nc.vector.scalar_tensor_tensor(out=y_lo[:, k, :], in0=bank[k // 2][:, (k % 2) * T:(k % 2 + 1) * T],
                                                   scalar=pcol[:, R_GQ + k:R_GQ + k + 1], in1=y_hi[:, k, :],
                                                   op0=ALU.mult, op1=ALU.subtract).then_inc(cq_lo.sem, 1)
                lo(l, S_UQ)
                lo(l, S_UQ + 1)
                mod_get(l, 1, mod_b)
                link(nc.vector.tensor_tensor(mod_b[:], mod_b[:], pcol[:, 16:40], ALU.add))
                coefficients(mod_b, R_N2)

                def pair_sums(kind, ss):
                    dve.wait_ge(psq_done.sem, psq_done.at(l, kind + 1))
                    nc.vector.tensor_reduce(ss, acc[:, 0:1024].rearrange("p (m d) -> p m d", d=HD), AX_X, ALU.add)\
                        .then_inc(pss_done.sem, 1)

                pair_sums(0, ss16)
                dve.wait_ge(cq_std.sem, cq_std.at(l, 2))
                nc.vector.reciprocal(ssc, ssc).then_inc(cq_rstd.sem, 1)

                dve.wait_ge(gains_in.sem, gains_in.at(l, 16 * 6))
                kr = proj[:, :, C_KR:C_KR + A_ROPE]
                half = A_ROPE // 2
                cos = konst[:, K_COS:K_COS + TT * A_ROPE].rearrange("p (t d) -> p t d", t=TT)
                sin = konst[:, K_SIN:K_SIN + TT * A_ROPE].rearrange("p (t d) -> p t d", t=TT)
                link(nc.vector.tensor_tensor(krw[:], kr, kr, ALU.mult))
                link(nc.vector.tensor_reduce(krss, krw[:], AX_X, ALU.add))
                link(nc.vector.tensor_tensor(kr, kr, gains[:, A_QK + A_NOPE:2 * A_QK].unsqueeze(1)
                                             .to_broadcast([P, TT, A_ROPE]), ALU.mult))
                nc.vector.tensor_tensor(krr[:], kr, cos, ALU.mult)
                nc.vector.tensor_tensor(krw[:, :, 0:half], kr[:, :, half:], sin[:, :, 0:half], ALU.mult)
                link(nc.vector.tensor_tensor(krw[:, :, half:], kr[:, :, 0:half], sin[:, :, half:], ALU.mult))
                link(nc.vector.tensor_tensor(krr[:], krr[:], krw[:], ALU.add))
                dve.sem_inc(kr_done.sem, 1)
                lo(l, S_UQ + 2)
                pair_sums(1, ss16b)

                def pair_norm(kind, base, ss, g0, fac):
                    dve.wait_ge(pstd_done.sem, pstd_done.at(l, kind + 1))
                    v = proj[:, :, base:base + 512].rearrange("p t (g d) -> p t g d", d=HD)
                    link(nc.vector.reciprocal(ss, ss))
                    link(nc.vector.tensor_tensor(ss, ss, konst[:, fac:fac + 16], ALU.mult))
                    for m in range(2):
                        gm = gains[:, g0 + HD * m:g0 + HD * (m + 1)].unsqueeze(1).unsqueeze(1)\
                            .to_broadcast([P, TT, 4, HD])
                        ins = nc.vector.tensor_tensor(v[:, :, 4 * m:4 * m + 4, :], v[:, :, 4 * m:4 * m + 4, :], gm,
                                                      ALU.mult)
                    link(ins)
                    nc.vector.tensor_tensor(v, v, ss.rearrange("p (t g) -> p t g", t=TT).unsqueeze(3)
                                            .to_broadcast([P, TT, 8, HD]), ALU.mult).then_inc(pn_done.sem, 1)

                pair_norm(0, C_C, ss16, 2 * A_QK + 2 * HD, K_FAC + 16)
                lo(l, S_UKV)

                for h in range(IDX_HEADS):
                    dve.wait_ge(relu_done.sem, relu_done.at(l, h + 1))
                    if h:
                        dve.wait_ge(idx_acc.sem, idx_acc.at(l, 2 * h))
                    for t, (c0, c1) in enumerate(((0, P), (P, P + T))):
                        wt = proj[:, t, C_IW + h:C_IW + h + 1]
                        if h == 0:
                            ins = nc.vector.tensor_scalar(score[:, c0:c1], relu_b[h % 4][:, c0:c1], wt, None, ALU.mult)
                        else:
                            ins = nc.vector.scalar_tensor_tensor(out=score[:, c0:c1], in0=relu_b[h % 4][:, c0:c1],
                                                                 scalar=wt, in1=score[:, c0:c1], op0=ALU.mult,
                                                                 op1=ALU.add)
                        ins.then_inc(idx_acc.sem, 1)
                    if h == 7:
                        pair_norm(1, C_B, ss16b, 2 * A_QK, K_FAC)
                        lo(l, S_GATE1)
                    if h == 11:
                        lo(l, S_GATE1 + 1)
                dve.wait_ge(idx_acc.sem, idx_acc.at(l, 2 * IDX_HEADS))
                link(nc.vector.scalar_tensor_tensor(out=score[:], in0=score[:], scalar=IDX_SCALE, in1=causal,
                                                    op0=ALU.mult, op1=ALU.add))

                def top_keys(t, rounds):
                    v = score[:, 0:P] if t == 0 else score[:, P:P + T]
                    for _ in range(rounds):
                        apart(dve)
                        link(nc.vector.max(top8, v))
                        apart(dve)
                        link(nc.vector.match_replace(v, top8, v, TAKEN))

                def k_rows(kind):
                    dve.wait_ge(pair_tp.sem, pair_tp.at(l, kind + 1))
                    for e in range(2):
                        q = slice(HD * e, HD * (e + 1))
                        nc.vector.tensor_copy(kz_t[q, 4 * kind + e:4 * kind + 4:2, :],
                                              bank[5 + 2 * kind][q, :].rearrange("p (a t) -> p a t", a=2))\
                            .then_inc(kz_out.sem, 1)

                k_rows(0)
                k_rows(1)
                lo(l, S_GATE1 + 2)

                dve.wait_ge(msq_done.sem, msq_done.at(l, 1))
                nc.vector.tensor_reduce(ss16, sq.rearrange("p (m d) -> p m d", d=A_QK), AX_X, ALU.add)\
                    .then_inc(mss_done.sem, 1)
                qv = q_a.rearrange("p (m d) -> p m d", d=A_QK)
                q4 = q_a.rearrange("p (t h d) -> p t h d", t=TT, h=A_HEADS)
                link(nc.vector.tensor_tensor(qv, qv, gains[:, 0:A_QK].unsqueeze(1).to_broadcast([P, 16, A_QK]), ALU.mult))
                rot = q4[:, :, :, A_NOPE:A_QK]
                ra = acc[:, 1536:2048].rearrange("p (t h d) -> p t h d", t=TT, h=A_HEADS)
                rb = acc[:, 2048:2560].rearrange("p (t h d) -> p t h d", t=TT, h=A_HEADS)
                nc.vector.tensor_tensor(ra, rot, cos.unsqueeze(2).to_broadcast([P, TT, A_HEADS, A_ROPE]), ALU.mult)
                nc.vector.tensor_tensor(rb[:, :, :, 0:half], rot[:, :, :, half:], sin[:, :, 0:half].unsqueeze(2)
                                        .to_broadcast([P, TT, A_HEADS, half]), ALU.mult)
                link(nc.vector.tensor_tensor(rb[:, :, :, half:], rot[:, :, :, 0:half], sin[:, :, half:].unsqueeze(2)
                                             .to_broadcast([P, TT, A_HEADS, half]), ALU.mult))
                link(nc.vector.tensor_tensor(rot, ra, rb, ALU.add))
                dve.wait_ge(msq_done.sem, msq_done.at(l, 2))
                link(nc.vector.tensor_reduce(ss16b, acc[:, 0:1024].rearrange("p (m d) -> p m d", d=A_NOPE), AX_X,
                                             ALU.add))
                sb3 = ss16b.rearrange("p (t h) -> p t h", t=TT)
                nc.vector.tensor_tensor(sb3, sb3, krss.unsqueeze(2).to_broadcast([P, TT, A_HEADS]), ALU.add)\
                    .then_inc(mss_done.sem, 1)
                lo(l, S_GATE1 + 3)
                dve.wait_ge(mstd_done.sem, mstd_done.at(l, 1))
                link(nc.vector.reciprocal(ss16, ss16))
                link(nc.vector.tensor_scalar(ss16, ss16, float(A_QK ** -0.5), None, ALU.mult))
                nc.vector.tensor_tensor(qv, qv, ss16.unsqueeze(2).to_broadcast([P, 16, A_QK]), ALU.mult)\
                    .then_inc(mqk_done.sem, 1)
                kv = k_a.rearrange("p (t h d) -> p t h d", t=TT, h=A_HEADS)
                link(nc.vector.tensor_tensor(kv[:, :, :, 0:A_NOPE], k_nope, gains[:, A_QK:A_QK + A_NOPE].unsqueeze(1)
                                             .unsqueeze(1).to_broadcast([P, TT, A_HEADS, A_NOPE]), ALU.mult))
                dve.wait_ge(mstd_done.sem, mstd_done.at(l, 2))
                link(nc.vector.reciprocal(ss16b, ss16b))
                nc.vector.tensor_tensor(kv[:, :, :, 0:A_NOPE], kv[:, :, :, 0:A_NOPE],
                                        sb3.unsqueeze(3).to_broadcast([P, TT, A_HEADS, A_NOPE]), ALU.mult)
                nc.vector.tensor_tensor(kv[:, :, :, A_NOPE:], krr[:].unsqueeze(2).to_broadcast([P, TT, A_HEADS, A_ROPE]),
                                        sb3.unsqueeze(3).to_broadcast([P, TT, A_HEADS, A_ROPE]), ALU.mult)\
                    .then_inc(mqk_done.sem, 1)
                for g in range(4, 7):
                    lo(l, S_GATE1 + g)
                for kind in range(2):
                    dve.wait_ge(mla_tp.sem, mla_tp.at(l, kind + 1))
                    for b in range(2, 4):
                        m = A_HEADS * kind + 2 * b
                        nc.vector.tensor_copy(qk_t[0:A_QK, m:m + 2, :].rearrange("p a t -> p (a t)"),
                                              bank[4 + b][0:A_QK, :]).then_inc(mla_out_d.sem, 1)
                    if kind == 0:
                        lo(l, S_GATE1 + 7)

                def scores_max(n):
                    kind, h = HEADS[n]
                    mask = {"a": causal, "b": neg_dist, "c": sel_nd[:]}[kind]
                    slope = head_slope(kind, h)
                    dve.wait_ge(scored.sem, scored.at(l, n + 1))
                    if n >= 4:
                        dve.wait_ge(p_tp.sem, p_tp.at(l, n - 3))
                    apart(dve)
                    for t, (c0, c1) in enumerate(((0, P), (P, P + T))):
                        nc.vector.tensor_tensor_reduce(p_sb[n % 4][:, c0:c1], bank[4 + n % 2][:, c0:c1], mask[:, c0:c1],
                                                       1.0, NEG, ALU.add, ALU.max, rowmax[n % 2][:, t:t + 1])\
                            .then_inc(ttr_done.sem, 1)
                    dve.wait_ge(ttr_done.sem, ttr_done.at(l, 2 * n + 2))
                    nc.vector.tensor_scalar(negmax[n % 2], rowmax[n % 2], -slope, None, ALU.mult)\
                        .then_inc(maxed.sem, 1)

                def normalize(n):
                    dve.wait_ge(exped.sem, exped.at(l, 2 * n + 2))
                    link(nc.vector.reciprocal(rinv[n % 2], rowsum[n % 2]))
                    for t, (c0, c1) in enumerate(((0, P), (P, P + T))):
                        ins = nc.vector.tensor_scalar(p_sb[n % 4][:, c0:c1], p_sb[n % 4][:, c0:c1],
                                                      rinv[n % 2][:, t:t + 1], None, ALU.mult)
                    ins.then_inc(p_ready.sem, 1)

                for n in range(NH + 5):
                    if n < NH:
                        scores_max(n)
                    if 1 <= n <= NH:
                        normalize(n - 1)
                    if 5 <= n < NH + 4 and n % 2:
                        pair = (n - 5) // 2
                        dve.wait_ge(y_hi_done.sem, y_hi_done.at(l, pair + 1))
                        nc.vector.tensor_tensor(y_lo[:, PAIR_Y[pair], :], bank[2 + pair % 2][:, 0:T],
                                                y_hi[:, PAIR_Y[pair], :], ALU.subtract).then_inc(y_lo_done.sem, 1)
                    if n - 2 in GATE_AT:
                        lo(l, gate_slab_no(GATE_AT[n - 2]) + 2)
                    for step in range(2 * n, 2 * n + 2) if n < 5 else range(n + 5, n + 6):
                        if step < 16:
                            top_keys(step // 8, 1)
                    if n == 11:
                        link(nc.vector.tensor_scalar(score[:], score[:], TAKEN / 2, NEG, ALU.is_ge, ALU.mult))
                        link(nc.vector.tensor_tensor(sel_nd[:], score[:], neg_dist, ALU.add))

                for hf in range(2):
                    banks = BR_BANKS[hf]
                    for m in range(2):
                        lo(l, S_BR + 2 + 2 * hf + m)
                    dve.wait_ge(slab_used.sem, slab_used.at(l, S_BR + 2 * hf + 1))
                    for q in range(2):
                        nc.vector.scalar_tensor_tensor(out=merged(hf)[:, 512 * q:512 * (q + 1)], in0=gate(2 * hf + q),
                                                       scalar=1.0, in1=bank[banks[0] + q][:, :], op0=ALU.add,
                                                       op1=ALU.mult).then_inc(m_first.sem, 1)
                    dve.wait_ge(m_first.sem, m_first.at(l, 2 * hf + 2))
                    dve.wait_ge(slab_used.sem, slab_used.at(l, S_BR + 2 * hf + 2))
                    for q in range(2):
                        g = 2 * hf + q
                        m_ = merged(hf)[:, 512 * q:512 * (q + 1)]
                        dst = [m_, gate(4 + g), gate(8 + g)]
                        for br in (1, 2):
                            ins = nc.vector.scalar_tensor_tensor(out=dst[br], in0=gate(4 * br + g), scalar=1.0,
                                                                 in1=bank[banks[br] + q][:, :], op0=ALU.add,
                                                                 op1=ALU.mult)
                        link(ins)
                        link(nc.vector.tensor_tensor(m_, m_, dst[1], ALU.add))
                        nc.vector.tensor_tensor(m_, m_, dst[2], ALU.add).then_inc(m_done.sem, 1)
                    for q in range(2):
                        k = 4 * hf + 2 * q
                        dve.wait_ge(m_hi.sem, m_hi.at(l, 2 * hf + q + 1))
                        nc.vector.scalar_tensor_tensor(out=h_lo[:, k:k + 2, :].rearrange("p a t -> p (a t)"),
                                                       in0=merged(hf)[:, 512 * q:512 * (q + 1)], scalar=0.5,
                                                       in1=h_hi[:, k:k + 2, :].rearrange("p a t -> p (a t)"),
                                                       op0=ALU.mult, op1=ALU.subtract).then_inc(m_lo.sem, 1)
                lo(l, S_OUT + 2)
                lo(l, S_OUT + 3)
                for ch in range(2):
                    lo(l, S_OUT + 4 + ch)
                    dve.wait_ge(slab_used.sem, slab_used.at(l, S_OUT + 3 + ch))
                    for k in range(4 * ch, 4 * ch + 4):
                        nc.vector.scalar_tensor_tensor(out=x_t[:, k, :], in0=bank[(6, 0)[ch] + k // 2 % 2][:, (k % 2) * T:(k % 2 + 1) * T],
                                                       scalar=mod_b[:, k:k + 1], in1=x_t[:, k, :], op0=ALU.mult,
                                                       op1=ALU.add).then_inc(x_done.sem, 1)
                norm(l, 1)

                def glu_step(par, i):
                    dve.wait_ge(silu_done.sem, silu_done.at(l, i + 1))
                    nc.vector.tensor_tensor(glu[par], silu_g[par], bank[5 + 2 * par][:, :], ALU.mult)\
                        .then_inc(glu_done.sem, 1)
                    dve.wait_ge(glu_hi_done.sem, glu_hi_done.at(l, i + 1))
                    nc.vector.tensor_tensor(glu_lo[par], glu[par], glu_hi[par], ALU.subtract)\
                        .then_inc(glu_lo_done.sem, 1)

                lo(l, S_FF + 2)
                glu_step(0, 0)
                lo(l, S_FF + 3)
                lo(l, S_FF + 4)
                lo(l, S_FF + 5)
                glu_step(1, 1)
                lo(l, S_FF + 6)
                dve.wait_ge(acc_zero.sem, acc_zero.at(l, 2))
                apart(dve)
                with dve.Fori(0, FF_PAIRS) as b:
                    pick_cond(l, b, b + 5, 2 * b + KT)
                    for e in range(2):
                        lo(l, S_FFL + 3 * e + 2, b)
                        lo(l, S_FFL + 3 * e + 3, b)
                        glu_step(e, 2 * b + (e + 2))
                        lo(l, S_FFL + 3 * e + 4, b)
                        m = 2 * b + (e + KT)
                        ada_step(l, m, ada_in[e].at(l, 32 * (b + 1) + 16 * (KT // 2)), e)
                lo(l, S_FFE + 2)
                lo(l, S_FFE + 3)
                glu_step(0, FG - 1)
                mod_get(l, 2, mod_a)
                link(nc.vector.tensor_tensor(mod_a[:, 0:8], mod_a[:, 0:8], pcol[:, 40:48], ALU.add))
                dve.wait_ge(slab_used.sem, slab_used.at(l, NS))
                for k in range(KT):
                    nc.vector.scalar_tensor_tensor(out=x_t[:, k, :], in0=bank[k // 2][:, (k % 2) * T:(k % 2 + 1) * T],
                                                   scalar=mod_a[:, k:k + 1], in1=x_t[:, k, :], op0=ALU.mult,
                                                   op1=ALU.add).then_inc(x_done.sem, 1)
                assert link.n == DVE_LINKS, link.n


_INS = ["x", "c", "w_ada", "b_ada", "norm1", "w_in", "g_cq", "w_uq", "g_ckv", "w_ukv", "qn_mla", "kn_mla", "qn_moba",
        "kn_moba", "qn_dsa", "kn_dsa", "w_br_a", "w_br_b", "w_br_c", "w_out", "norm2", "w_gu", "w_down"]


def kernel(**inputs):
    import concourse.bacc as bacc
    from concourse.bass_utils import run_bass_kernel_spmd

    nc = bacc.Bacc("TRN2", target_bir_lowering=False, num_devices=1)
    arrays = {f"in_{n}_dram": np.ascontiguousarray(inputs[n]) for n in _INS}
    arrays["in_const_dram"] = constants()
    args = [nc.dram_tensor(n, a.shape, mybir.dt.from_np(a.dtype), kind="ExternalInput").ap() for n, a in arrays.items()]
    out = nc.dram_tensor("out_0_dram", (1, T, D), F32, kind="ExternalOutput").ap()
    build(nc, *args, out)
    r = run_bass_kernel_spmd(nc, [arrays], core_ids=[0])
    return r.results[0]["out_0_dram"]
```
